# Optimizing a Trainium2 kernel written in Bass

```python
import math
import jax, jax.numpy as jnp
from jax import lax
import numpy as np

D_MODEL = 1024
BATCH = 1
SEQ = 1024
DEPTH = 2

N_META = 16
BLOCK_Q = 128
PAD = BLOCK_Q - N_META
HG_WIDTH = D_MODEL // 2
HG_HEADS = 4
HG_DK = HG_WIDTH // HG_HEADS
HG_DV = HG_WIDTH // HG_HEADS
HG_CHUNK = 64
DA_WIDTH = D_MODEL // 4
DA_HEADS = 4
DA_DV = DA_WIDTH // DA_HEADS
DA_DQK = DA_DV // 2
FX_WIDTH = D_MODEL // 4
FX_HEADS = 4
FX_DH = FX_WIDTH // FX_HEADS
MIX_WIDTH = HG_WIDTH + DA_WIDTH + FX_WIDTH
IN_SIZES = (HG_WIDTH, HG_WIDTH, HG_WIDTH, HG_WIDTH,
            DA_WIDTH, DA_WIDTH, DA_WIDTH,
            FX_WIDTH, FX_WIDTH, FX_WIDTH, FX_HEADS)
IN_WIDTH = sum(IN_SIZES)
N_GROUPS = 4
EXPERTS_PER_GROUP = 8
N_EXPERTS = N_GROUPS * EXPERTS_PER_GROUP
TOP_K = 2
D_EXPERT = D_MODEL // 2
MOE_BLOCK = 128
ROPE_THETA = 10000.0
EPS = 1e-6
NEG = -1e30
TINY = 1e-30

kernel_name = "hymba_hgrn2_diff_fox_hmoe"

def _rmsnorm(x, g):
    x32 = x.astype(jnp.float32)
    y = x32 * lax.rsqrt(jnp.mean(x32 * x32, axis=-1, keepdims=True) + EPS)
    return (y * g.astype(jnp.float32)).astype(x.dtype)

def _rope(x, pos):
    d = x.shape[-1]
    inv = ROPE_THETA ** (-jnp.arange(0, d, 2, dtype=jnp.float32) / d)
    ang = pos.astype(jnp.float32)[:, None] * inv[None, :]
    cos, sin = jnp.cos(ang), jnp.sin(ang)
    x32 = x.astype(jnp.float32)
    x1, x2 = x32[..., : d // 2], x32[..., d // 2:]
    return jnp.concatenate([x1 * cos - x2 * sin, x2 * cos + x1 * sin], axis=-1).astype(x.dtype)

def _to_heads(t, n):
    b, l, _ = t.shape
    return t.reshape(b, l, n, -1).transpose(0, 2, 1, 3)

def _hgrn2(q, fz, i, g, lb, gain, valid):
    b, l, _ = q.shape
    f32 = jnp.float32
    z = fz.astype(f32)
    lb = lb.astype(f32)
    sig = jax.nn.sigmoid(z)
    f = lb + (1.0 - lb) * sig
    log_f = jnp.log(jnp.maximum(f, TINY))
    k = (1.0 - lb) * (1.0 - sig)
    m = valid[None, :, None]
    log_f = jnp.where(m, log_f, 0.0)
    k = jnp.where(m, k, 0.0)
    qs = jax.nn.silu(q.astype(f32)) * (HG_DK ** -0.5)
    n_chunks = l // HG_CHUNK

    def chunks(t):
        return _to_heads(t, HG_HEADS).reshape(b, HG_HEADS, n_chunks, HG_CHUNK, -1).transpose(2, 0, 1, 3, 4)

    qc, kc, vc, gc = chunks(qs), chunks(k), chunks(i.astype(f32)), chunks(log_f)
    causal = jnp.tril(jnp.ones((HG_CHUNK, HG_CHUNK), dtype=bool))[:, :, None]

    def step(S, inp):
        qt, kt, vt, gt = inp
        G = jnp.cumsum(gt, axis=-2)
        o_inter = jnp.einsum('bhtk,bhkv->bhtv', qt * jnp.exp(G), S)
        rel = jnp.where(causal, G[:, :, :, None, :] - G[:, :, None, :, :], 0.0)
        decay = jnp.where(causal, jnp.exp(rel), 0.0)
        A = jnp.einsum('bhtk,bhsk,bhtsk->bhts', qt, kt, decay)
        o = o_inter + jnp.einsum('bhts,bhsv->bhtv', A, vt)
        G_last = G[:, :, -1:, :]
        S = jnp.exp(G_last[:, :, 0, :, None]) * S + jnp.einsum('bhsk,bhsv->bhkv', kt * jnp.exp(G_last - G), vt)
        return S, o

    S0 = jnp.zeros((b, HG_HEADS, HG_DK, HG_DV), f32)
    _, o = lax.scan(step, S0, (qc, kc, vc, gc))
    o = o.transpose(1, 0, 3, 2, 4).reshape(b, l, HG_HEADS, HG_DV).astype(q.dtype)
    o = _rmsnorm(o, gain) * jax.nn.silu(g).reshape(b, l, HG_HEADS, HG_DV)
    return o.reshape(b, l, HG_WIDTH)

def _diff_attn(q, k, v, lam_vecs, gain, lam_init, pos, valid):
    b, l, _ = q.shape
    nb = l // BLOCK_Q
    q = _rope(_to_heads(q, 2 * DA_HEADS), pos).reshape(b, DA_HEADS, 2, l, DA_DQK)
    k = _rope(_to_heads(k, 2 * DA_HEADS), pos).reshape(b, DA_HEADS, 2, l, DA_DQK)
    v = _to_heads(v, DA_HEADS)
    lv = lam_vecs.astype(jnp.float32)
    lam = jnp.exp(jnp.sum(lv[0] * lv[1])) - jnp.exp(jnp.sum(lv[2] * lv[3])) + lam_init
    qb = q.reshape(b, DA_HEADS, 2, nb, BLOCK_Q, DA_DQK).transpose(3, 0, 1, 2, 4, 5)
    key_idx = jnp.arange(l)
    scale = DA_DQK ** -0.5

    def block(args):
        qi, bi = args
        s = jnp.einsum('bhcqd,bhckd->bhcqk', qi, k).astype(jnp.float32) * scale
        q_idx = bi * BLOCK_Q + jnp.arange(BLOCK_Q)
        mask = (key_idx[None, :] <= q_idx[:, None]) & valid[None, :]
        p = jax.nn.softmax(jnp.where(mask, s, NEG), axis=-1)
        w = (p[:, :, 0] - lam * p[:, :, 1]).astype(v.dtype)
        return jnp.einsum('bhqk,bhkv->bhqv', w, v)

    o = lax.map(block, (qb, jnp.arange(nb)))
    o = o.transpose(1, 0, 3, 2, 4).reshape(b, l, DA_HEADS, DA_DV)
    o = _rmsnorm(o, gain) * (1.0 - lam_init)
    return o.reshape(b, l, DA_WIDTH)

def _fox_attn(q, k, v, fz, bias, gain, valid):
    b, l, _ = q.shape
    nb = l // BLOCK_Q
    q, k, v = _to_heads(q, FX_HEADS), _to_heads(k, FX_HEADS), _to_heads(v, FX_HEADS)
    log_f = jax.nn.log_sigmoid(fz.astype(jnp.float32) + bias.astype(jnp.float32))
    D = jnp.cumsum(log_f, axis=1).transpose(0, 2, 1)
    qb = q.reshape(b, FX_HEADS, nb, BLOCK_Q, FX_DH).transpose(2, 0, 1, 3, 4)
    db = D.reshape(b, FX_HEADS, nb, BLOCK_Q).transpose(2, 0, 1, 3)
    key_idx = jnp.arange(l)
    scale = FX_DH ** -0.5

    def block(args):
        qi, di, bi = args
        s = jnp.einsum('bhqd,bhkd->bhqk', qi, k).astype(jnp.float32) * scale
        s = s + di[..., :, None] - D[:, :, None, :]
        q_idx = bi * BLOCK_Q + jnp.arange(BLOCK_Q)
        mask = (key_idx[None, :] <= q_idx[:, None]) & valid[None, :]
        p = jax.nn.softmax(jnp.where(mask, s, NEG), axis=-1).astype(v.dtype)
        return jnp.einsum('bhqk,bhkv->bhqv', p, v)

    o = lax.map(block, (qb, db, jnp.arange(nb)))
    o = o.transpose(1, 0, 3, 2, 4).reshape(b, l, FX_HEADS, FX_DH)
    return _rmsnorm(o, gain).reshape(b, l, FX_WIDTH)

def _hier_moe(u, w_group, b_group, w_router, b_router, w1, w3, w2):
    b, l, d = u.shape
    n = b * l
    h = u.reshape(n, d)
    g_logits = (h @ w_group).astype(jnp.float32) + b_group.astype(jnp.float32)
    p_group = jax.nn.softmax(g_logits, axis=-1)
    g_sel = jnp.argmax(g_logits, axis=-1)
    p_gsel = jnp.take_along_axis(p_group, g_sel[:, None], axis=1)
    e_logits = ((h @ w_router).astype(jnp.float32) + b_router.astype(jnp.float32)).reshape(n, N_GROUPS, EXPERTS_PER_GROUP)
    e_in = jnp.take_along_axis(e_logits, g_sel[:, None, None], axis=1)[:, 0]
    top_p, top_i = lax.top_k(jax.nn.softmax(e_in, axis=-1), TOP_K)
    gate = p_gsel * top_p / jnp.sum(top_p, axis=-1, keepdims=True)
    expert = g_sel[:, None] * EXPERTS_PER_GROUP + top_i

    a = n * TOP_K
    e_flat = expert.reshape(a).astype(jnp.int32)
    t_flat = jnp.repeat(jnp.arange(n, dtype=jnp.int32), TOP_K)
    w_flat = gate.reshape(a)
    order = jnp.argsort(e_flat)
    e_s, t_s, w_s = e_flat[order], t_flat[order], w_flat[order]
    counts = jnp.bincount(e_flat, length=N_EXPERTS)
    padded = (counts + MOE_BLOCK - 1) // MOE_BLOCK * MOE_BLOCK
    start = jnp.cumsum(counts) - counts
    p_end = jnp.cumsum(padded)
    p_start = p_end - padded
    dest = p_start[e_s] + jnp.arange(a, dtype=jnp.int32) - start[e_s]
    p_rows = ((a + MOE_BLOCK - 1) // MOE_BLOCK + N_EXPERTS) * MOE_BLOCK
    tok_buf = jnp.full((p_rows,), n, dtype=jnp.int32).at[dest].set(t_s)
    w_buf = jnp.zeros((p_rows,), jnp.float32).at[dest].set(w_s)
    n_blocks = p_rows // MOE_BLOCK
    blk_expert = jnp.minimum(jnp.searchsorted(p_end, jnp.arange(n_blocks, dtype=jnp.int32) * MOE_BLOCK, side='right'), N_EXPERTS - 1)
    x_pad = jnp.concatenate([h, jnp.zeros((1, d), h.dtype)], axis=0)

    def run(args):
        tok, e = args
        xb = x_pad[tok]
        return (jax.nn.silu(xb @ w1[e]) * (xb @ w3[e])) @ w2[e]

    y = lax.map(run, (tok_buf.reshape(n_blocks, MOE_BLOCK), blk_expert))
    out = jnp.zeros((n + 1, d), h.dtype).at[tok_buf].add(y.reshape(p_rows, d) * w_buf[:, None].astype(h.dtype))
    return out[:n].reshape(b, l, d)

def setup_inputs(seed: int = 0) -> dict:
    key = jax.random.key(seed)
    ks = jax.random.split(key, 20)
    nrm = jax.random.normal
    f32 = jnp.float32
    return {
        "x": nrm(ks[0], (BATCH, SEQ, D_MODEL), f32),
        "meta_tokens": nrm(ks[1], (N_META, D_MODEL), f32),
        "norm_mix": 1.0 + 0.02 * nrm(ks[2], (DEPTH, D_MODEL), f32),
        "w_in": nrm(ks[3], (DEPTH, D_MODEL, IN_WIDTH), f32) * D_MODEL ** -0.5,
        "hgrn_lb": 0.5 * nrm(ks[4], (DEPTH, HG_WIDTH), f32),
        "hgrn_norm": 1.0 + 0.02 * nrm(ks[5], (DEPTH, HG_DV), f32),
        "diff_lambda": 0.1 * nrm(ks[6], (DEPTH, 4, DA_DQK), f32),
        "diff_norm": 1.0 + 0.02 * nrm(ks[7], (DEPTH, DA_DV), f32),
        "fox_bias": 3.0 + 0.1 * nrm(ks[8], (DEPTH, FX_HEADS), f32),
        "fox_norm": 1.0 + 0.02 * nrm(ks[9], (DEPTH, FX_DH), f32),
        "w_out": nrm(ks[10], (DEPTH, MIX_WIDTH, D_MODEL), f32) * MIX_WIDTH ** -0.5,
        "norm_ffn": 1.0 + 0.02 * nrm(ks[11], (DEPTH, D_MODEL), f32),
        "w_group": nrm(ks[12], (DEPTH, D_MODEL, N_GROUPS), f32) * D_MODEL ** -0.5,
        "b_group": 0.01 * nrm(ks[13], (DEPTH, N_GROUPS), f32),
        "w_router": nrm(ks[14], (DEPTH, D_MODEL, N_EXPERTS), f32) * D_MODEL ** -0.5,
        "b_router": 0.01 * nrm(ks[15], (DEPTH, N_EXPERTS), f32),
        "w1": nrm(ks[16], (DEPTH, N_EXPERTS, D_MODEL, D_EXPERT), f32) * D_MODEL ** -0.5,
        "w3": nrm(ks[17], (DEPTH, N_EXPERTS, D_MODEL, D_EXPERT), f32) * D_MODEL ** -0.5,
        "w2": nrm(ks[18], (DEPTH, N_EXPERTS, D_EXPERT, D_MODEL), f32) * D_EXPERT ** -0.5,
        "norm_final": 1.0 + 0.02 * nrm(ks[19], (D_MODEL,), f32),
    }

def reference(x, meta_tokens, norm_mix, w_in, hgrn_lb, hgrn_norm, diff_lambda, diff_norm,
              fox_bias, fox_norm, w_out, norm_ffn, w_group, b_group, w_router, b_router,
              w1, w3, w2, norm_final):
    b = x.shape[0]
    pad = jnp.zeros((b, PAD, D_MODEL), x.dtype)
    meta = jnp.broadcast_to(meta_tokens.astype(x.dtype)[None], (b, N_META, D_MODEL))
    h = jnp.concatenate([pad, meta, x], axis=1)
    l = h.shape[1]
    idx = jnp.arange(l)
    pos = idx - PAD
    valid = idx >= PAD
    s_lb = jax.nn.softmax(hgrn_lb.astype(jnp.float32), axis=0)
    lb_all = jnp.cumsum(s_lb, axis=0) - s_lb[0]
    split_at = np.cumsum(IN_SIZES)[:-1].tolist()
    for layer in range(DEPTH):
        u = _rmsnorm(h, norm_mix[layer])
        proj = u @ w_in[layer]
        hq, hf, hi, hg, dq, dk, dv, fq, fk, fv, ff = jnp.split(proj, split_at, axis=-1)
        lam_init = 0.8 - 0.6 * math.exp(-0.3 * layer)
        o_a = _hgrn2(hq, hf, hi, hg, lb_all[layer], hgrn_norm[layer], valid)
        o_b = _diff_attn(dq, dk, dv, diff_lambda[layer], diff_norm[layer], lam_init, pos, valid)
        o_c = _fox_attn(fq, fk, fv, ff, fox_bias[layer], fox_norm[layer], valid)
        h = h + jnp.concatenate([o_a, o_b, o_c], axis=-1) @ w_out[layer]
        u = _rmsnorm(h, norm_ffn[layer])
        h = h + _hier_moe(u, w_group[layer], b_group[layer], w_router[layer], b_router[layer],
                          w1[layer], w3[layer], w2[layer])
    h = _rmsnorm(h, norm_final)
    return h[:, PAD + N_META:]


_drawn_inputs = setup_inputs


def setup_inputs(seed=0):
    import zlib

    import numpy as np

    out = dict(_drawn_inputs(seed))
    spreads = {}
    factors = {'b_group': 3.755, 'b_router': 3.046, 'norm_final': 2.835}
    for name, (base, spread) in spreads.items():
        noise = np.random.default_rng([zlib.crc32(name.encode()), seed]).standard_normal(out[name].shape)
        drawn = base * np.exp(spread * noise) if base else spread * noise
        out[name] = __import__('jax').numpy.asarray(drawn.astype(out[name].dtype))
    for name, factor in factors.items():
        out[name] = (out[name] * factor).astype(out[name].dtype)
    return out
```

```python
import math
from contextlib import ExitStack

import numpy as np

import concourse.bass as bass
from concourse import mybir

F32 = mybir.dt.float32
I32 = mybir.dt.int32
ALU = mybir.AluOpType
ACT = mybir.ActivationFunctionType
AX = mybir.AxisListType

D = 1024
SEQ = 1024
DEPTH = 2
META = 16
L = META + SEQ
P = 128
T = 1 + SEQ // P
KD = D // P
HEADS = 4
HW = 128
AW = 64
DQK = AW // 2
BAND_DA = HEADS * 4 * HW
BAND_FX = BAND_DA + HEADS * 2 * AW
BAND_V = BAND_FX + HEADS * 2 * AW
BAND_FF = BAND_V + 2 * HEADS * AW
GROUPS = 4
PER_GROUP = 8
EXPERTS = GROUPS * PER_GROUP
ROUTES = GROUPS + EXPERTS
F = D // 2
KF = F // P
EPS = 1e-6
TINY = 1e-30
NEG = -1e30
BLOCKS = (EXPERTS + (2 * L - EXPERTS) // P + 1) // 2 * 2
LEVELS = [64, 32, 16, 8, 4, 2, 1]
NL = len(LEVELS) + 1
MEETINGS = 8
ONE = 1


def rows(j):
    return META if j == 0 else P


def cols(j):
    return slice(0, META) if j == 0 else slice(META + P * (j - 1), META + P * j)


def chunks(n):
    return [(a, min(a + 512, n)) for a in range(0, n, 512)]


def groups_of(j):
    return [list(range(a, min(a + 4, j + 1))) for a in range(0, j + 1, 4)]


class Steps:

    def __init__(self, engine, semaphore, every):
        self.engine, self.semaphore, self.every = engine, semaphore, every

    def begin(self, turn):
        self.turn, self.n = turn, 0
        self.last = (self.semaphore, ONE + turn * self.every)

    def made(self, instruction):
        self.n += 1
        instruction.then_inc(self.semaphore, 1)
        self.last = (self.semaphore, ONE + self.turn * self.every + self.n)

    def after(self, semaphore, value):
        self.last = (semaphore, ONE + value)

    def settle(self):
        self.engine.wait_ge(*self.last)

    def end(self):
        assert self.n == self.every, (self.semaphore, self.n, self.every)


def build(nc, A, out, stop=MEETINGS, depth=DEPTH):
    nc.disable_value_cache = True
    with ExitStack() as ctx:
        def sb(name, shape, dt=F32):
            return ctx.enter_context(nc.sbuf_tensor(name, shape, dt))

        from_one = []

        def signal(name):
            return ctx.enter_context(nc.semaphore(name))

        def sem(name):
            from_one.append(signal(name))
            return from_one[-1]

        h = sb("h", [P, T, D])
        ident = sb("ident", [P, P])
        causal = sb("causal", [P, P])
        gamma = sb("gamma", [P, D])
        gain_hg = sb("gain_hg", [P, DEPTH, HW])
        gain_da = sb("gain_da", [P, DEPTH, AW])
        gain_fx = sb("gain_fx", [P, DEPTH, AW])
        lb = sb("lb", [P, DEPTH, HEADS])
        rest = sb("rest", [P, DEPTH, HEADS])
        lbt = sb("lbt", [P, 3, HEADS])
        lamv = sb("lamv", [P, DEPTH, 4, DQK])
        lamp = sb("lamp", [P, DEPTH, 2, DQK])
        lams = sb("lams", [P, DEPTH, 2])
        lam_init = sb("lam_init", [P, DEPTH, 2])
        neglam = sb("neglam", [P, DEPTH])
        neglam_l = sb("neglam_l", [P, 1])
        fbias = sb("fbias", [HEADS, DEPTH])
        eps = sb("eps", [P, 1])
        ss = sb("ss", [P, T])
        lnss = sb("lnss", [P, T])
        rstd = sb("rstd", [P, T])
        negmax = sb("negmax", [P, 2 * T])
        rowsum = sb("rowsum", [P, 2 * T])
        rinv = sb("rinv", [P, 2 * T])
        rneg = sb("rneg", [P, T])
        glast = sb("glast", [P, T])
        dest = sb("dest", [P, 2, T], I32)
        gate = sb("gate", [P, 2, T])
        pairs = sb("pairs", [1, 2], I32)
        pairs_f = sb("pairs_f", [1, 2])
        blk_expert = sb("blk_expert", [1, BLOCKS], I32)

        ARENA = 41472
        arena = sb("arena", [P, ARENA])
        uT = arena[:, 0:KD * L].rearrange("p (k n) -> p k n", k=KD)
        mix = arena[:, KD * L:KD * L + T * D].rearrange("p (j d) -> p j d", j=T)
        SCRATCH = KD * L + T * D

        class Place:
            def __init__(self, at):
                self.at = at

            def take(self, *shape, parts=P):
                n = int(np.prod(shape))
                assert self.at + n <= ARENA, (self.at + n, ARENA)
                v = arena[0:parts, self.at:self.at + n]
                self.at += n
                if len(shape) == 2:
                    v = v.rearrange("p (a b) -> p a b", a=shape[0])
                if len(shape) == 3:
                    v = v.rearrange("p (a b c) -> p a b c", a=shape[0], b=shape[1])
                return v

        junk = arena[:, SCRATCH:SCRATCH + 2 * D].rearrange("p (s d) -> p s d", s=2)

        s = Place(SCRATCH)
        w_fq = s.take(KD, 2 * HW)
        w_ig = s.take(KD, 2 * HW)
        masks = s.take(NL, P)
        reset = s.take(L)
        QK = s.take(len(LEVELS), L)
        hq = s.take(L)
        hk = s.take(L)
        hG = s.take(L)
        hX = [s.take(L), s.take(L)]
        hQ = s.take(L)
        hK = s.take(L)
        ig = s.take(T, 2 * HW)
        AT = s.take(2, P)
        KtT = s.take(2, P)
        S = s.take(2, P)
        x_at, k_at, q_at = (s.at - 3 * 2 * P - T * 2 * HW) - 4 * L, 0, 0
        oh = arena[:, x_at:x_at + T * HW].rearrange("p (j v) -> p j v", j=T)
        osq = arena[:, x_at - 2 * L:x_at - 2 * L + T * HW].rearrange("p (j v) -> p j v", j=T)
        eg = arena[:, x_at + 2 * L:x_at + 2 * L + T * HW].rearrange("p (j v) -> p j v", j=T)

        s = Place(SCRATCH)
        w_v = s.take(KD, 2 * HEADS * AW)
        w_qk = s.take(KD, 2 * AW)
        w_ff = s.take(KD, HEADS)
        cos = s.take(L)
        sin = s.take(L)
        swap = s.take(P)
        raw = s.take(L)
        rot = s.take(L)
        qT = s.take(L)
        kT = s.take(L)
        Pr = s.take(2, L)
        PT = s.take(2, T, P)
        V = s.take(T, 2 * HEADS * AW)
        ah = s.take(T, AW)
        asq = s.take(T, AW)

        s = Place(SCRATCH + 2 * D)
        w_o = s.take(KD, D)
        mT = s.take(2, KD, P)

        s = Place(SCRATCH)
        w_r = s.take(KD, ROUTES)
        ones = s.take(P)
        earlier = s.take(P)
        b_r = s.take(ROUTES)
        valid = s.take(T)
        first4 = s.take(GROUPS)
        first8 = s.take(PER_GROUP)
        blk_no = s.take(BLOCKS)
        lg = s.take(T, ROUTES)
        gm = s.take(T)
        g4 = s.take(T, GROUPS)
        ohg = s.take(T, GROUPS)
        psel = s.take(T)
        big = s.take(T, EXPERTS)
        ein = s.take(T, PER_GROUP)
        m1 = s.take(T)
        m2 = s.take(T)
        t8 = s.take(T, PER_GROUP)
        o1 = s.take(T, PER_GROUP)
        o2 = s.take(T, PER_GROUP)
        tm = s.take(T)
        E = [s.take(T, EXPERTS), s.take(T, EXPERTS)]
        both = s.take(T, EXPERTS)
        tot = s.take(EXPERTS)
        cnt_i = s.take(EXPERTS).bitcast(I32)
        nblk = s.take(EXPERTS)
        upto = s.take(EXPERTS)
        base = s.take(EXPERTS)
        place = s.take(T, EXPERTS)
        destf = s.take(2, T)
        cmp = s.take(BLOCKS, EXPERTS)
        blkf = s.take(BLOCKS)
        zero32 = s.take(EXPERTS)

        s = Place(0)
        W1 = [s.take(KD, F), s.take(KD, F)]
        W3 = [s.take(KD, F), s.take(KD, F)]
        W2 = [s.take(KF, D), s.take(KF, D)]
        xb = s.take(2, D)
        XT = s.take(KD, P)
        sg = s.take(F)
        G = s.take(F)
        GT = s.take(KF, P)
        yb = s.take(2, D)

        s = Place(0)
        ya = s.take(2, 2, D)

        ps = ctx.enter_context(nc.psum_tensor("ps", [P, 8, 512], F32))
        flat = ps[:, :, :].rearrange("p b n -> p (b n)")
        bigps = [flat[:, 0:1536], flat[:, 1536:3072]]

        xg = nc.dram_tensor("xg", (BLOCKS * P + P, D), F32, kind="Internal").ap()
        decay_rows = nc.dram_tensor("decay_rows", (2, HEADS, L), F32, kind="Internal").ap()

        met, passed = signal("met"), signal("passed")
        s_start, s_par, s_x0 = signal("s_start"), signal("s_par"), signal("s_x0")
        s_init, s_initd = signal("s_init"), signal("s_initd")
        s_zero, s_zfill = signal("s_zero"), signal("s_zfill")
        s_gamma, s_clean = signal("s_gamma"), signal("s_clean")
        v_init = sem("v_init")
        n_rstd, n_u, n_tp, n_ua, n_uv, n_act = [], [], [], [], [], []
        for which in ("mixn", "ffnn", "last"):
            n_rstd.append(sem(which + "_rstd"))
            n_u.append(sem(which + "_u"))
            n_act.append(sem(which + "_act"))
            n_tp.append(sem(which + "_tp"))
            n_ua.append(sem(which + "_ua"))
            n_uv.append(sem(which + "_uv"))
        h_const, h_wfq, h_wig = signal("h_const"), signal("h_wfq"), signal("h_wig")
        h_f, h_q, h_ig, h_igc = sem("h_f"), sem("h_q"), sem("h_ig"), sem("h_igc")
        h_gexp, h_clamped, h_logf, h_diff = sem("h_gexp"), sem("h_clamped"), sem("h_logf"), sem("h_diff")
        h_decay, h_factor, h_glast = sem("h_decay"), sem("h_factor"), sem("h_glast")
        h_lvl, h_at, h_ktT, h_ktTc = sem("h_lvl"), sem("h_at"), sem("h_ktT"), sem("h_ktTc")
        h_o, h_oc, h_ds, h_S = sem("h_o"), sem("h_oc"), sem("h_ds"), sem("h_S")
        h_eg, h_ss, h_rstd, h_out = sem("h_eg"), sem("h_ss"), sem("h_rstd"), sem("h_out")
        h_v, h_a = sem("h_v"), sem("h_a")
        class Attention:
            def __init__(self, kind, maps):
                self.maps, self.U = maps, maps * T
                self.w, self.drow = signal(f"{kind}_w"), signal(f"{kind}_drow")
                self.proj, self.raw, self.perm = sem(f"{kind}_proj"), sem(f"{kind}_raw"), sem(f"{kind}_perm")
                self.qk, self.qd, self.S = sem(f"{kind}_qk"), sem(f"{kind}_qd"), sem(f"{kind}_S")
                self.max, self.P, self.TP = sem(f"{kind}_max"), sem(f"{kind}_P"), sem(f"{kind}_TP")
                self.ptA, self.ptV = sem(f"{kind}_ptA"), sem(f"{kind}_ptV")
                self.pv, self.oc = sem(f"{kind}_pv"), sem(f"{kind}_oc")
                self.ss, self.rstd, self.out = sem(f"{kind}_ss"), sem(f"{kind}_rstd"), sem(f"{kind}_out")
                self.v, self.a = sem(f"{kind}_v"), sem(f"{kind}_a")

        da, fx = Attention("da", 2), Attention("fx", 1)
        v_w, v_p, v_c = signal("v_w"), sem("v_p"), sem("v_c")
        f_w, f_st = signal("f_w"), signal("f_st")
        f_p, f_x, f_act, f_l, f_d, f_v = (sem(n) for n in ("f_p", "f_x", "f_act", "f_l", "f_d", "f_v"))
        p_w = signal("p_w")
        p_tp, p_ta, p_tv, p_mm, p_h = (sem(n) for n in ("p_tp", "p_ta", "p_tv", "p_mm", "p_h"))
        r_w, r_sc = signal("r_w"), signal("r_sc")
        r_lg, r_v, r_exp, r_m, r_rank, r_cnt, r_dest, r_A, r_tot = (sem(n) for n in (
            "r_lg", "r_v", "r_exp", "r_m", "r_rank", "r_cnt", "r_dest", "r_A", "r_tot"))
        m_x = [signal("m_x0"), signal("m_x1")]
        m_w13 = [signal("m_w13_0"), signal("m_w13_1")]
        m_w2 = [signal("m_w2_0"), signal("m_w2_1")]
        m_xt, m_xtc, m_h, m_e, m_v, m_g, m_gt, m_gtc, m_ya, m_yv = (sem(n) for n in (
            "m_xt", "m_xtc", "m_h", "m_e", "m_v", "m_g", "m_gt", "m_gtc", "m_ya", "m_yv"))
        m_up, m_y = [sem("m_up0"), sem("m_up1")], [sem("m_y0"), sem("m_y1")]
        m_out = [signal("m_out0"), signal("m_out1")]
        c_y = [signal("c_y0"), signal("c_y1")]
        c_h, c_v = sem("c_h"), sem("c_v")
        s_store = signal("s_store")

        block = ctx.enter_context(nc.Block())
        ENG = 5

        def wait_alone(engine, semaphore, value):
            engine.wait_ge(semaphore, value)
            engine.sem_inc(passed, 1)

        def meet(engine, layer, phase):
            engine.sem_inc(passed, 1)
            engine.drain().then_inc(met, 1)
            wait_alone(engine, met, (layer * MEETINGS + phase + 1) * ENG)

        CLEANS = 9

        @block.sync
        def _(sp):
            def load_gamma(row):
                sp.dma_start(gamma[:, :], row.partition_broadcast(P)).then_inc(s_gamma, 16)

            sp.dma_start(ident[:, :], A["c_ident"]).then_inc(s_start, 16)
            sp.dma_start(h[0:META, 0, :], A["meta_tokens"]).then_inc(s_x0, 16)
            for j in range(1, T):
                sp.dma_start(h[:, j, :], A["x"][0, P * (j - 1):P * j, :]).then_inc(s_x0, 16)
            for dst, src in (
                (causal[:, :], A["c_causal"]),
                (gain_hg[:, :, :], A["hgrn_norm"].partition_broadcast(P)),
                (gain_da[:, :, :], A["diff_norm"].partition_broadcast(P)),
                (gain_fx[:, :, :], A["fox_norm"].partition_broadcast(P)),
                (lb[:, :, :], A["hgrn_lb"]),
                (lamv[:, :, :, :], A["diff_lambda"].partition_broadcast(P)),
                (lam_init[:, :, :], A["c_lam_init"].partition_broadcast(P)),
                (fbias[:, :], A["fox_bias"]),
            ):
                sp.dma_start(dst, src).then_inc(s_par, 16)

            with sp.Fori(0, depth) as layer:
                load_gamma(A["norm_mix"][layer])
                meet(sp, layer, 0)
                if stop > 1:
                    load_gamma(A["norm_ffn"][layer])
                    sp.dma_start(masks, A["c_masks"]).then_inc(h_const, 16)
                    sp.dma_start(reset, A["c_reset"].partition_broadcast(P)).then_inc(h_const, 16)
                    with sp.Fori(0, HEADS) as head:
                        t = layer * HEADS + head
                        w = A["w_in"][layer].rearrange("(p k) c -> p k c", k=KD)
                        wait_alone(sp, h_q, ONE + t)
                        sp.dma_start(w_fq, w[:, :, bass.ds(head * 4 * HW, 2 * HW)]).then_inc(h_wfq, 16)
                        wait_alone(sp, h_ig, ONE + t * T)
                        sp.dma_start(w_ig, w[:, :, bass.ds(head * 4 * HW + 2 * HW, 2 * HW)]).then_inc(h_wig, 16)
                    meet(sp, layer, 1)
                if stop > 2:
                    w = A["w_in"][layer].rearrange("(p k) c -> p k c", k=KD)
                    sp.dma_start(w_v, w[:, :, BAND_V:BAND_FF]).then_inc(v_w, 16)
                    sp.dma_start(w_ff, w[:, :, BAND_FF:BAND_FF + HEADS]).then_inc(f_w, 16)
                    for dst, src in ((cos, "c_cos"), (sin, "c_sin"), (swap, "c_swap")):
                        sp.dma_start(dst, A[src]).then_inc(v_w, 16)
                    with sp.Fori(0, HEADS) as head:
                        t = layer * HEADS + head
                        w = A["w_in"][layer].rearrange("(p k) c -> p k c", k=KD)
                        wait_alone(sp, da.proj, ONE + t)
                        sp.dma_start(w_qk, w[:, :, bass.ds(head * 2 * AW + BAND_DA, 2 * AW)]).then_inc(da.w, 16)
                    meet(sp, layer, 2)
                if stop > 3:
                    wait_alone(sp, f_d, ONE + layer * 2 + 2)
                    sp.dma_start(decay_rows[0], raw[0:HEADS]).then_inc(f_st, 16)
                    sp.dma_start(decay_rows[1], rot[0:HEADS]).then_inc(f_st, 16)
                    wait_alone(sp, f_st, layer * 32 + 32)
                    with sp.Fori(0, HEADS) as head:
                        t = layer * HEADS + head
                        w = A["w_in"][layer].rearrange("(p k) c -> p k c", k=KD)
                        wait_alone(sp, fx.proj, ONE + t)
                        sp.dma_start(w_qk, w[:, :, bass.ds(head * 2 * AW + BAND_FX, 2 * AW)]).then_inc(fx.w, 16)
                        wait_alone(sp, fx.S, ONE + t * T)
                        sp.dma_start(kT[AW:AW + 1], decay_rows[0, bass.ds(head, 1)]).then_inc(fx.drow, 16)
                        sp.dma_start(qT[AW + 1:AW + 2], decay_rows[1, bass.ds(head, 1)]).then_inc(fx.drow, 16)
                    meet(sp, layer, 3)
                if stop > 4:
                    sp.dma_start(w_o, A["w_out"][layer].rearrange("(k p) c -> p k c", p=P)).then_inc(p_w, 16)
                    meet(sp, layer, 4)
                if stop > 5:
                    sp.dma_start(w_r, A["w_route"][layer].rearrange("(p k) c -> p k c", k=KD)).then_inc(r_w, 16)
                    sp.dma_start(b_r, A["b_route"][layer].partition_broadcast(P)).then_inc(r_w, 16)
                    for dst, src in ((earlier, "c_earlier"), (valid, "c_valid"), (first4, "c_first4"), (first8, "c_first8"),
                                     (blk_no, "c_blk_no")):
                        sp.dma_start(dst, A[src]).then_inc(r_w, 16)
                    meet(sp, layer, 5)
                if stop > 6:
                    before = sp.value_load(pairs[0:1, 1:2], min_val=0, max_val=BLOCKS // 2)
                    count = sp.value_load(pairs[0:1, 0:1], min_val=1, max_val=BLOCKS // 2)
                    with sp.Fori(0, count) as i:
                        t = before + i
                        for k in range(2):
                            e = sp.value_load(blk_expert[0:1, bass.ds(i * 2 + k, 1)], min_val=0,
                                              max_val=EXPERTS - 1)
                            wait_alone(sp, m_up[k], ONE + t)
                            sp.dma_start(W1[k], A["w1"][layer, e].rearrange("(p k) f -> p k f", k=KD))\
                              .then_inc(m_w13[k], 16)
                            sp.dma_start(W3[k], A["w3"][layer, e].rearrange("(p k) f -> p k f", k=KD))\
                              .then_inc(m_w13[k], 16)
                            wait_alone(sp, m_y[k], ONE + t)
                            sp.dma_start(W2[k], A["w2"][layer, e].rearrange("(j p) d -> p j d", p=P))\
                              .then_inc(m_w2[k], 16)
                    meet(sp, layer, 6)
                if stop > 7:
                    meet(sp, layer, 7)

            if stop >= MEETINGS:
                load_gamma(A["norm_final"])
                for j in range(1, T):
                    sp.wait_ge(n_u[2], ONE + j)
                    sp.dma_start(out[0, P * (j - 1):P * j, :], mix[:, j, :]).then_inc(s_store, 16)
                sp.wait_ge(s_store, 16 * (T - 1))

        @block.scalar
        def _(act):
            nc.scalar.preload_act_table_set("natural_log_exp_and_others")

            steps = [Steps(act, n_act[0], 2 * T), Steps(act, n_act[1], 2 * T), Steps(act, n_act[2], 2 * (T - 1))]

            def norm_stats(which, turn, j, count=T, first=0):
                r, st = rows(j), steps[which]
                st.made(act.activation(junk[0:r, 0, :], h[0:r, j, :], ACT.Square, accum_out=ss[0:r, j:j + 1]))
                st.settle()
                st.made(act.activation(lnss[0:r, j:j + 1], ss[0:r, j:j + 1], ACT.Ln, bias=eps[0:r, :],
                                       scale=1.0 / D))
                st.settle()
                act.activation(rstd[0:r, j:j + 1], lnss[0:r, j:j + 1], ACT.Exp, scale=-0.5)\
                   .then_inc(n_rstd[which], 1)

            def norm_copy(which, turn, j):
                r = rows(j)
                act.wait_ge(n_tp[which], ONE + turn * 2 * T + 2 * j + 1)
                act.activation(uT[:, 0:4, cols(j)], ps[:, 2, :].rearrange("p (k n) -> p k n", k=4)[:, :, 0:r],
                               ACT.Copy).then_inc(n_ua[which], 1)

            act.wait_ge(s_initd, 1)
            act.activation(lbt[:, 0, :], lbt[:, 0, :], ACT.Exp).then_inc(s_init, 1)
            act.activation(lbt[:, 1, :], lbt[:, 1, :], ACT.Exp).then_inc(s_init, 1)
            act.wait_ge(s_initd, 2)
            act.activation(lams[:, :, :], lams[:, :, :], ACT.Exp).then_inc(s_init, 1)

            def attend_act(a, layer, head, turn):
                U = a.U
                groups = sum(len(groups_of(j)) for j in range(T))
                if a is da:
                    act.wait_ge(a.proj, ONE + turn + 1)
                    act.wait_ge(a.qk, ONE + turn)
                    act.activation(raw, bigps[0][:, 0:L], ACT.Copy).then_inc(a.raw, 1)
                else:
                    act.wait_ge(a.proj, ONE + turn + 1)
                    act.wait_ge(a.S, ONE + turn * U)
                    act.activation(kT[0:AW], bigps[0][AW:2 * AW, 0:L], ACT.Copy).then_inc(a.qk, 1)

                def turned(u):
                    return groups * (u // T) + sum(len(groups_of(j)) for j in range(u % T + 1)) if u >= 0 else 0

                def probs(u):
                    c, j = divmod(u, T)
                    r, n = rows(j), META + P * j
                    act.wait_ge(a.max, ONE + turn * U + u + 1)
                    act.wait_ge(a.TP, ONE + turn * groups * a.maps + turned(u - 2))
                    act.activation(Pr[0:r, u % 2, 0:n], bigps[j % 2][0:r, 0:n], ACT.Exp,
                                   bias=negmax[0:r, u:u + 1], accum_out=rowsum[0:r, u:u + 1]).then_inc(a.P, 1)

                def evacuate(u):
                    c, j = divmod(u, T)
                    g0 = groups_of(j)[0]
                    act.wait_ge(a.TP, ONE + turn * groups * a.maps + turned(u) - len(groups_of(j)) + 1)
                    act.wait_ge(a.pv, ONE + turn * U + max(u - 1, 0))
                    bank = 6 + (turned(u) - len(groups_of(j))) % 2
                    act.activation(PT[:, u % 2, 0:len(g0), 0:rows(j)],
                                   ps[:, bank, 0:len(g0) * P].rearrange("p (i n) -> p i n", i=len(g0))[:, :, 0:rows(j)],
                                   ACT.Copy).then_inc(a.ptA, 1)

                probs(0)
                for u in range(U):
                    if u + 1 < U:
                        probs(u + 1)
                    evacuate(u)
                head_rstd(a.ss, a.a, a.rstd, turn, AW)

            def head_rstd(ready, own, done, turn, width):
                act.wait_ge(ready, ONE + turn + 1)
                act.activation(lnss[:, :], ss[:, :], ACT.Ln, bias=eps[:, :], scale=1.0 / width).then_inc(own, 1)
                act.wait_ge(own, ONE + turn + 1)
                act.activation(rstd[:, :], lnss[:, :], ACT.Exp, scale=-0.5).then_inc(done, 1)

            with act.Fori(0, depth) as layer:
                act.wait_ge(s_x0, 16 * T)
                act.wait_ge(s_initd, 5)
                steps[0].begin(layer)
                for j in range(T + 1):
                    if j < T:
                        norm_stats(0, layer, j)
                    if j >= 1:
                        norm_copy(0, layer, j - 1)
                steps[0].end()
                meet(act, layer, 0)

                if stop > 1:
                    wait_alone(act, s_clean, layer * CLEANS + 2)
                    with act.Fori(0, HEADS) as head:
                        t = layer * HEADS + head

                        def copy_ig(j):
                            r = rows(j)
                            act.wait_ge(h_ig, ONE + t * T + j + 1)
                            if j == 0:
                                act.wait_ge(h_o, ONE + t * T)
                                act.wait_ge(h_ds, ONE + t * (T - 1))
                                act.wait_ge(h_out, ONE + t)
                            act.activation(ig[0:r, j, :], ps[0:r, 6 + j % 2, 0:2 * HW], ACT.Copy).then_inc(h_igc, 1)

                        act.wait_ge(h_f, ONE + t + 1)
                        act.wait_ge(h_out, ONE + t)
                        act.wait_ge(h_ktT, ONE + t * (T - 1))
                        act.activation(hK, bigps[1][:, 0:L], ACT.Exp, scale=-1.0).then_inc(h_gexp, 1)
                        act.wait_ge(h_q, ONE + t + 1)
                        act.wait_ge(h_o, ONE + t * T)
                        act.activation(hQ, bigps[0][:, 0:L], ACT.Exp, scale=-1.0).then_inc(h_gexp, 1)
                        copy_ig(0)
                        act.wait_ge(h_clamped, ONE + t + 1)
                        act.activation(hX[1], hX[0], ACT.Ln).then_inc(h_logf, 1)
                        copy_ig(1)
                        act.wait_ge(h_diff, ONE + t * 9 + 1)
                        act.activation(hX[0], hG, ACT.Exp).then_inc(h_decay, 1)
                        act.activation(glast[:, :], hG[:, META - 1:L:P], ACT.Exp).then_inc(h_glast, 1)
                        copy_ig(2)
                        for i in range(1, 9):
                            act.wait_ge(h_diff, ONE + t * 9 + i + 1)
                            act.activation(hX[i % 2], hX[i % 2], ACT.Exp).then_inc(h_decay, 1)
                            if i + 2 < T:
                                copy_ig(i + 2)
                        for j in range(T):
                            r = rows(j)
                            if j < T - 1:
                                act.wait_ge(h_ktT, ONE + t * (T - 1) + j + 1)
                                act.wait_ge(h_ds, ONE + t * (T - 1) + max(j - 1, 0))
                                act.activation(KtT[0:r, j % 2, :], ps[0:r, 2, 0:P], ACT.Copy).then_inc(h_ktTc, 1)
                            act.wait_ge(h_o, ONE + t * T + j + 1)
                            if j == 0:
                                act.wait_ge(h_factor, ONE + t * 9 + 9)
                            act.activation(oh[0:r, j, :], ps[0:r, 5, 0:HW], ACT.Copy).then_inc(h_oc, 1)
                        act.activation(eg, ig[:, :, HW:2 * HW], ACT.Exp, scale=-1.0).then_inc(h_eg, 1)
                        head_rstd(h_ss, h_a, h_rstd, t, HW)
                    meet(act, layer, 1)

                if stop > 2:
                    act.wait_ge(s_clean, layer * CLEANS + 7)
                    for j in range(T):
                        act.wait_ge(v_p, ONE + layer * T + j + 1)
                        act.activation(V[0:rows(j), j, :], ps[0:rows(j), 3 + j % 2, :], ACT.Copy).then_inc(v_c, 1)
                    with act.Fori(0, HEADS) as head:
                        attend_act(da, layer, head, layer * HEADS + head)
                    meet(act, layer, 2)

                if stop > 3:
                    fl = Pr[0:HEADS, 0, :]
                    act.wait_ge(f_x, ONE + layer + 1)
                    act.activation(fl, raw[0:HEADS], ACT.Abs).then_inc(f_act, 1)
                    act.wait_ge(f_act, ONE + layer * 2 + 1)
                    act.activation(fl, fl, ACT.Exp, scale=-1.0).then_inc(f_act, 1)
                    act.wait_ge(f_act, ONE + layer * 2 + 2)
                    act.activation(fl, fl, ACT.Ln, bias=1.0).then_inc(f_l, 1)
                    with act.Fori(0, HEADS) as head:
                        attend_act(fx, layer, head, layer * HEADS + head)
                    meet(act, layer, 3)

                if stop > 4:
                    steps[1].begin(layer)

                    def copy_mT(j):
                        act.wait_ge(p_tp, ONE + layer * 2 * T + 2 * j + 1)
                        act.wait_ge(p_mm, ONE + layer * T + max(j - 1, 0))
                        act.activation(mT[:, j % 2, 0:4, 0:rows(j)],
                                       ps[:, 6, :].rearrange("p (k n) -> p k n", k=4)[:, :, 0:rows(j)],
                                       ACT.Copy).then_inc(p_ta, 1)

                    copy_mT(0)
                    for j in range(T):
                        if j + 1 < T:
                            copy_mT(j + 1)
                        act.wait_ge(p_h, ONE + layer * T + j + 1)
                        norm_stats(1, layer, j)
                        if j >= 1:
                            norm_copy(1, layer, j - 1)
                    norm_copy(1, layer, T - 1)
                    steps[1].end()
                    meet(act, layer, 4)

                if stop > 5:
                    act.wait_ge(r_m, ONE + layer * 2 + 1)
                    act.activation(g4, g4, ACT.Exp).then_inc(r_exp, 1)
                    act.wait_ge(r_m, ONE + layer * 2 + 2)
                    act.activation(tm, tm, ACT.Exp).then_inc(r_exp, 1)
                    meet(act, layer, 5)

                if stop > 6:
                    before = act.value_load(pairs[0:1, 1:2], min_val=0, max_val=BLOCKS // 2)
                    count = act.value_load(pairs[0:1, 0:1], min_val=1, max_val=BLOCKS // 2)
                    act.wait_ge(m_xt, ONE + before * 4 + layer * 2)
                    act.dma_start(xb[:, 0, :], xg[0:P, :]).then_inc(m_x[0], 16)
                    act.wait_ge(m_xt, ONE + before * 4 + layer * 2 + 2)
                    act.activation(XT[:, 0:4, :].rearrange("p k n -> p (k n)"), ps[:, 5, :], ACT.Copy)\
                       .then_inc(m_xtc, 1)
                    with act.Fori(0, count) as i:
                        t = before + i
                        for k in range(2):
                            nxt = 1 - k
                            act.wait_ge(m_xt, ONE + t * 4 + 2 * k + 2 * layer)
                            act.dma_start(xb[:, nxt, :], xg[bass.ds((i * 2 + k + 1) * P, P), :])\
                               .then_inc(m_x[nxt], 16)
                            act.wait_ge(m_h, ONE + t * 4 + 2 * k + 1)
                            act.wait_ge(m_g, ONE + t * 4 + 2 * k)
                            act.activation(sg, ps[:, 0, :], ACT.Exp, scale=-1.0).then_inc(m_e, 1)
                            act.wait_ge(m_xt, ONE + t * 4 + 2 * k + 2 * layer + 4 - 1)
                            act.activation(XT[:, 0:4, :].rearrange("p k n -> p (k n)"), ps[:, 5, :], ACT.Copy)\
                               .then_inc(m_xtc, 1)
                            for q in range(2):
                                act.wait_ge(m_gt, ONE + t * 4 + 2 * k + q + 1)
                                if q == 0:
                                    act.wait_ge(m_y[1 - k], ONE + t + k)
                                act.activation(GT[:, 2 * q:2 * q + 2, :].rearrange("p k n -> p (k n)"),
                                               ps[:, 7, 0:2 * P], ACT.Copy).then_inc(m_gtc, 1)
                            act.wait_ge(m_y[k], ONE + t + 1)
                            act.wait_ge(m_out[k], 16 + t * 16)
                            act.activation(yb[:, k, 0:512], ps[:, 3, :], ACT.Copy).then_inc(m_ya, 1)
                            act.wait_ge(m_ya, ONE + t * 2 + k + 1)
                            act.wait_ge(m_yv, ONE + t * 2 + k + 1)
                            act.dma_start(xg[bass.ds((i * 2 + k) * P, P), :], yb[:, k, :]).then_inc(m_out[k], 16)
                    act.wait_ge(m_out[0], 16 + (before + count) * 16)
                    act.wait_ge(m_out[1], 16 + (before + count) * 16)
                    act.activation(lnss[:, :], ss[:, :], ACT.Copy)
                    meet(act, layer, 6)

                if stop > 7:
                    meet(act, layer, 7)

            if stop >= MEETINGS:
                steps[2].begin(0)
                for j in range(1, T):
                    norm_stats(2, 0, j)
                steps[2].end()

        @block.tensor
        def _(pe):
            def norm_turn(which, turn, j):
                pe.wait_ge(n_u[which], ONE + turn * T + j + 1)
                pe.wait_ge(n_ua[which], ONE + turn * T + j)
                pe.wait_ge(n_uv[which], ONE + turn * T + j)
                for k in range(KD):
                    bank = 2 if k < 4 else 5
                    mm = pe.transpose(ps[:, bank, (k % 4) * P:(k % 4 + 1) * P], mix[:, j, k * P:(k + 1) * P],
                                      ident[:, :])
                    if k % 4 == 3:
                        mm.then_inc(n_tp[which], 1)

            pe.wait_ge(s_start, 16)

            def project(dst, w, lo, hi):
                for a, b in chunks(L):
                    for k in range(KD):
                        mm = pe.matmul(dst[0:hi - lo, a:b], w[:, k, lo:hi], uT[:, k, a:b],
                                       start=(k == 0), stop=(k == KD - 1))
                return mm

            def attend_pe(a, layer, head, turn):
                U = a.U
                groups = sum(len(groups_of(j)) for j in range(T))
                G0 = turn * groups * a.maps
                A0 = turn * U
                V0 = turn * 6 * a.maps
                pe.wait_ge(a.w, turn * 16 + 16)
                pe.wait_ge(a.P, ONE + A0)
                project(bigps[0], w_qk, 0, 2 * AW).then_inc(a.proj, 1)
                if a is da:
                    pe.wait_ge(a.raw, ONE + turn + 1)
                    pe.wait_ge(a.oc, ONE + A0)
                    for x, y in chunks(L):
                        mm = pe.matmul(bigps[1][:, x:y], swap[:, :], raw[:, x:y], start=True, stop=True)
                    mm.then_inc(a.perm, 1)
                    pe.wait_ge(a.qk, ONE + turn + 1)
                else:
                    pe.wait_ge(a.qk, ONE + turn + 1)
                    pe.wait_ge(a.qd, ONE + turn + 1)
                    pe.wait_ge(a.drow, turn * 32 + 32)

                last_use = {}
                evac = []
                na = nv = 0

                def scores(u):
                    c, j = divmod(u, T)
                    if j % 2 in last_use:
                        pe.wait_ge(a.P, ONE + A0 + last_use[j % 2] + 1)
                    last_use[j % 2] = u
                    r, n = rows(j), META + P * j
                    for x, y in chunks(n):
                        if a is da:
                            first = cols(j).start
                            lhs, rhs = qT[c * DQK:(c + 1) * DQK, first:first + P], kT[c * DQK:(c + 1) * DQK, x:y]
                        else:
                            first = cols(j).start
                            lhs, rhs = qT[0:AW + 2, first:first + P], kT[0:AW + 2, x:y]
                        mm = pe.matmul(bigps[j % 2][:, x:y], lhs, rhs, start=True, stop=True)
                    mm.then_inc(a.S, 1)

                scores(0)
                for u in range(U):
                    c, j = divmod(u, T)
                    r = rows(j)
                    if u + 1 < U:
                        scores(u + 1)
                    pe.wait_ge(a.P, ONE + A0 + u + 1)
                    for gi, g in enumerate(groups_of(j)):
                        n = len(evac)
                        if n >= 2:
                            pe.wait_ge(*evac[n - 2])
                        for i in g:
                            first = cols(i).start
                            mm = pe.transpose(ps[:, 6 + n % 2, (i - g[0]) * P:(i - g[0] + 1) * P],
                                              Pr[:, u % 2, first:first + P], ident[:, :])
                        mm.then_inc(a.TP, 1)
                        if gi == 0:
                            na += 1
                            evac.append((a.ptA, ONE + A0 + na))
                        else:
                            nv += 1
                            evac.append((a.ptV, ONE + V0 + nv))
                    pe.wait_ge(a.ptA, ONE + A0 + na)
                    if len(groups_of(j)) > 1:
                        pe.wait_ge(a.ptV, ONE + V0 + nv)
                    pe.wait_ge(a.oc, ONE + A0 + u)
                    at = 0 if a is da else HEADS * AW
                    for i in range(j + 1):
                        mm = pe.matmul(ps[:, 5, 0:AW], PT[:, u % 2, i, :],
                                       V[:, i, bass.ds(head * AW + at, AW)], start=(i == 0), stop=(i == j))
                    mm.then_inc(a.pv, 1)

            with pe.Fori(0, depth) as layer:
                for j in range(T):
                    norm_turn(0, layer, j)
                meet(pe, layer, 0)

                if stop > 1:
                    with pe.Fori(0, HEADS) as head:
                        t = layer * HEADS + head
                        pe.wait_ge(h_wfq, t * 16 + 16)
                        pe.wait_ge(h_at, ONE + t * T)
                        pe.wait_ge(h_oc, ONE + t * T)
                        project(bigps[1], w_fq, 0, HW).then_inc(h_f, 1)
                        pe.wait_ge(h_ktTc, ONE + t * (T - 1))
                        project(bigps[0], w_fq, HW, 2 * HW).then_inc(h_q, 1)
                        pe.wait_ge(h_wig, t * 16 + 16)
                        for j in range(T):
                            r = rows(j)
                            pe.wait_ge(h_igc, ONE + t * T + max(j - 1, 0))
                            if j == 1:
                                pe.wait_ge(h_S, ONE + t * (T - 1))
                            for k in range(KD):
                                mm = pe.matmul(ps[0:r, 6 + j % 2, 0:2 * HW], uT[:, k, cols(j)], w_ig[:, k, :],
                                               start=(k == 0), stop=(k == KD - 1))
                            mm.then_inc(h_ig, 1)

                        def levels(j):
                            r = rows(j)
                            if j == 0:
                                pe.wait_ge(h_factor, ONE + t * 9 + 8)
                            pe.wait_ge(h_at, ONE + t * T + max(j - 1, 0))
                            for li in range(NL):
                                if li < NL - 1 and LEVELS[li] >= r:
                                    continue
                                lhs = hk if li == NL - 1 else QK[:, li, :]
                                rhs = hq if li == NL - 1 else QK[:, li, :]
                                mm = pe.matmul(bigps[j % 2][0:r, li * P:li * P + r], lhs[:, cols(j)],
                                               rhs[:, cols(j)], start=True, stop=True)
                            mm.then_inc(h_lvl, 1)

                        levels(0)
                        for j in range(T):
                            r = rows(j)
                            if j + 1 < T:
                                levels(j + 1)
                            if j < T - 1:
                                if j == 0:
                                    pe.wait_ge(h_factor, ONE + t * 9 + 9)
                                pe.wait_ge(h_ktTc, ONE + t * (T - 1) + j)
                                pe.transpose(ps[0:r, 2, 0:P], hK[:, cols(j)], ident[:, :]).then_inc(h_ktT, 1)
                            pe.wait_ge(h_at, ONE + t * T + j + 1)
                            pe.wait_ge(h_igc, ONE + t * T + T)
                            pe.wait_ge(h_oc, ONE + t * T + j)
                            if j > 0:
                                pe.wait_ge(h_S, ONE + t * (T - 1) + j)
                                pe.matmul(ps[0:r, 5, 0:HW], hQ[:, cols(j)], S[:, (j - 1) % 2, :],
                                          start=True, stop=False)
                            pe.matmul(ps[:, 5, 0:HW], AT[0:r, j % 2, :], ig[0:r, j, 0:HW],
                                      start=(j == 0), stop=True).then_inc(h_o, 1)
                            if j < T - 1:
                                pe.wait_ge(h_ktTc, ONE + t * (T - 1) + j + 1)
                                pe.matmul(ps[:, 7, 0:HW], KtT[0:r, j % 2, :], ig[0:r, j, 0:HW],
                                          start=True, stop=True).then_inc(h_ds, 1)
                    meet(pe, layer, 1)

                if stop > 2:
                    pe.wait_ge(v_w, layer * 64 + 64)
                    for j in range(T):
                        pe.wait_ge(v_c, ONE + layer * T + max(j - 1, 0))
                        for k in range(KD):
                            mm = pe.matmul(ps[0:rows(j), 3 + j % 2, :], uT[:, k, cols(j)], w_v[:, k, :],
                                           start=(k == 0), stop=(k == KD - 1))
                        mm.then_inc(v_p, 1)
                    wait_alone(pe, v_c, ONE + layer * T + T)
                    with pe.Fori(0, HEADS) as head:
                        attend_pe(da, layer, head, layer * HEADS + head)
                    meet(pe, layer, 2)

                if stop > 3:
                    pe.wait_ge(f_w, layer * 16 + 16)
                    project(bigps[0], w_ff, 0, HEADS).then_inc(f_p, 1)
                    wait_alone(pe, f_x, ONE + layer + 1)
                    with pe.Fori(0, HEADS) as head:
                        attend_pe(fx, layer, head, layer * HEADS + head)
                    meet(pe, layer, 3)

                if stop > 4:
                    def turn_mix(j):
                        r = rows(j)
                        pe.wait_ge(p_ta, ONE + layer * T + j)
                        pe.wait_ge(p_tv, ONE + layer * T + j)
                        for k in range(KD):
                            mm = pe.transpose(ps[:, 6 + k // 4, (k % 4) * P:(k % 4 + 1) * P],
                                              mix[:, j, k * P:(k + 1) * P], ident[:, :])
                            if k % 4 == 3:
                                mm.then_inc(p_tp, 1)

                    turn_mix(0)
                    pe.wait_ge(p_w, layer * 16 + 16)
                    for j in range(T):
                        r = rows(j)
                        if j + 1 < T:
                            turn_mix(j + 1)
                        pe.wait_ge(p_ta, ONE + layer * T + j + 1)
                        pe.wait_ge(p_tv, ONE + layer * T + j + 1)
                        pe.wait_ge(p_h, ONE + layer * T + max(j - 1, 0))
                        for half in range(2):
                            for k in range(KD):
                                mm = pe.matmul(ps[0:r, 3 * (j % 2) + half, :], mT[:, j % 2, k, 0:r],
                                               w_o[:, k, half * 512:half * 512 + 512],
                                               start=(k == 0), stop=(k == KD - 1))
                        mm.then_inc(p_mm, 1)
                        if j >= 1:
                            norm_turn(1, layer, j - 1)
                    norm_turn(1, layer, T - 1)
                    meet(pe, layer, 4)

                if stop > 5:
                    pe.wait_ge(r_w, layer * 112 + 112)
                    for j in range(T):
                        for k in range(KD):
                            mm = pe.matmul(ps[0:rows(j), 0, j * ROUTES:(j + 1) * ROUTES], uT[:, k, cols(j)],
                                           w_r[:, k, :], start=(k == 0), stop=(k == KD - 1))
                    mm.then_inc(r_lg, 1)
                    pe.wait_ge(r_A, ONE + layer + 1)
                    W = T * EXPERTS
                    pe.matmul(ps[:, 1, 0:W], earlier[:, :], both.rearrange("p j e -> p (j e)"),
                              start=True, stop=False, skip_group_check=True)
                    for j in range(T - 1):
                        for i in range(j + 1, T):
                            mm = pe.matmul(ps[:, 1, i * EXPERTS:(i + 1) * EXPERTS], ones[:, :], both[:, j, :],
                                           start=False, stop=(j == T - 2), skip_group_check=True)
                    mm.then_inc(r_rank, 1)
                    pe.wait_ge(r_tot, ONE + layer + 1)
                    pe.matmul(ps[:, 2, 0:EXPERTS], ones[:, :], tot, start=True, stop=True).then_inc(r_cnt, 1)
                    meet(pe, layer, 5)

                if stop > 6:
                    before = pe.value_load(pairs[0:1, 1:2], min_val=0, max_val=BLOCKS // 2)
                    count = pe.value_load(pairs[0:1, 0:1], min_val=1, max_val=BLOCKS // 2)

                    def turn_rows(k):
                        for c in range(KD):
                            mm = pe.transpose(ps[:, 5 + c // 4, (c % 4) * P:(c % 4 + 1) * P],
                                              xb[:, k, c * P:(c + 1) * P], ident[:, :])
                            if c % 4 == 3:
                                mm.then_inc(m_xt, 1)

                    pe.wait_ge(m_x[0], before * 16 + layer * 16 + 16)
                    turn_rows(0)
                    with pe.Fori(0, count) as i:
                        t = before + i
                        for k in range(2):
                            pe.wait_ge(m_xtc, ONE + t * 4 + 2 * k + 2 * layer + 2)
                            pe.wait_ge(m_w13[k], t * 32 + 32)
                            pe.wait_ge(m_g, ONE + t * 4 + 2 * k)
                            for c in range(KD):
                                mm = pe.matmul(ps[:, 0, :], XT[:, c, :], W1[k][:, c, :],
                                               start=(c == 0), stop=(c == KD - 1))
                            mm.then_inc(m_h, 1)
                            for q in range(2):
                                for c in range(KD):
                                    mm = pe.matmul(ps[:, 1 + q, 0:F // 2], XT[:, c, :],
                                                   W3[k][:, c, q * F // 2:(q + 1) * F // 2],
                                                   start=(c == 0), stop=(c == KD - 1))
                                mm.then_inc(m_h if q == 0 else m_up[k], 1)
                            if k == 0:
                                pe.wait_ge(m_x[1], t * 16 + 16)
                            else:
                                pe.wait_ge(m_x[0], t * 16 + layer * 16 + 32)
                            turn_rows(1 - k)
                            pe.wait_ge(m_w2[k], t * 16 + 16)
                            pe.wait_ge(m_ya, ONE + t * 2 + k)
                            pe.wait_ge(m_yv, ONE + t * 2 + k)
                            for q in range(2):
                                pe.wait_ge(m_g, ONE + t * 4 + 2 * k + q + 1)
                                pe.wait_ge(m_gtc, ONE + t * 4 + 2 * k + q)
                                for c in range(2):
                                    f0 = (2 * q + c) * P
                                    mm = pe.transpose(ps[:, 7, c * P:(c + 1) * P], G[:, f0:f0 + P], ident[:, :])
                                mm.then_inc(m_gt, 1)
                                pe.wait_ge(m_gtc, ONE + t * 4 + 2 * k + q + 1)
                                for half in range(2):
                                    for c in range(2 * q, 2 * q + 2):
                                        mm = pe.matmul(ps[:, 3 + half, :], GT[:, c, :],
                                                       W2[k][:, c, half * 512:half * 512 + 512],
                                                       start=(c == 0), stop=(c == KF - 1))
                            mm.then_inc(m_y[k], 1)
                    meet(pe, layer, 6)

                if stop > 7:
                    meet(pe, layer, 7)

        @block.gpsimd
        def _(pool):
            for semaphore in from_one:
                pool.sem_inc(semaphore, ONE)
            for semaphore in m_out:
                pool.sem_inc(semaphore, 16)
            wait_alone(pool, s_zero, 1)
            for b in range(BLOCKS + 1):
                pool.dma_start(xg[b * P:(b + 1) * P, :], junk[:, 1, :]).then_inc(s_zfill, 16)
            with pool.Fori(0, depth) as layer:
                for phase in range(min(5, stop)):
                    meet(pool, layer, phase)
                if stop > 5:
                    wait_alone(pool, s_zfill, 16 * (BLOCKS + 1))
                    wait_alone(pool, r_dest, ONE + layer + 1)
                    for k in range(2):
                        for j in range(T):
                            pool.indirect_dma_start(
                                out=xg[:, :], out_offset=bass.IndirectOffsetOnAxis(ap=dest[0:rows(j), k, j:j + 1], axis=0),
                                in_=mix[0:rows(j), j, :], in_offset=None).then_inc(r_sc, 16)
                    wait_alone(pool, r_sc, layer * 32 * T + 32 * T)
                    meet(pool, layer, 5)
                if stop > 6:
                    meet(pool, layer, 6)
                if stop > 7:
                    for j in range(T):
                        wait_alone(pool, c_h, ONE + layer * T + max(j - 1, 0))
                        for k in range(2):
                            pool.indirect_dma_start(
                                out=ya[0:rows(j), j % 2, k, :], out_offset=None, in_=xg[:, :],
                                in_offset=bass.IndirectOffsetOnAxis(ap=dest[0:rows(j), k, j:j + 1], axis=0))\
                                .then_inc(c_y[j % 2], 16)
                    meet(pool, layer, 7)

        @block.vector
        def _(v):
            def norm_apply(which, turn, j, count=T):
                r = rows(j)
                v.wait_ge(n_rstd[which], ONE + turn * T + j + (1 if which < 2 else 0))
                perm = "p (n k) -> p k n"
                v.scalar_tensor_tensor(
                    out=mix[0:r, j, :].rearrange("p (k n) -> p k n", k=KD) if which < 2 else mix[0:r, j, :],
                    in0=h[0:r, j, :].rearrange(perm, k=KD) if which < 2 else h[0:r, j, :],
                    scalar=rstd[0:r, j:j + 1],
                    in1=gamma[0:r, :].rearrange(perm, k=KD) if which < 2 else gamma[0:r, :],
                    op0=ALU.mult, op1=ALU.mult).then_inc(n_u[which], 1)

            def norm_copy(which, turn, j):
                v.wait_ge(n_tp[which], ONE + turn * 2 * T + 2 * j + 2)
                v.tensor_copy(uT[:, 4:8, cols(j)], ps[:, 5, :].rearrange("p (k n) -> p k n", k=4)[:, :, 0:rows(j)])\
                 .then_inc(n_uv[which], 1)

            v.memset(junk[:, 1, :], 0.0).then_inc(s_zero, 1)
            v.memset(eps[:, :], EPS)
            v.memset(pairs_f[:, :], 0.0)
            v.memset(arena[:, KD * L:KD * L + D], 0.0)
            v.memset(ss[:, :], 1.0)
            v.memset(negmax[:, :], 0.0)
            v.memset(rowsum[:, :], 1.0)
            v.memset(flat[:, 3072:4096], 0.0)
            st = Steps(v, v_init, 15)
            st.begin(0)
            v.wait_ge(s_par, 16 * 8)
            st.made(v.tensor_tensor(lbt[:, 2, :], lb[:, 0, :], lb[:, 1, :], ALU.max))
            st.settle()
            st.made(v.tensor_tensor(lbt[:, 0, :], lb[:, 0, :], lbt[:, 2, :], ALU.subtract))
            v.tensor_tensor(lbt[:, 1, :], lb[:, 1, :], lbt[:, 2, :], ALU.subtract).then_inc(s_initd, 1)
            st.made(v.tensor_tensor(lamp[:, :, :, :], lamv[:, :, 0:4:2, :], lamv[:, :, 1:4:2, :], ALU.mult))
            st.settle()
            v.tensor_reduce(lams[:, :, :], lamp[:, :, :, :], AX.X, ALU.add).then_inc(s_initd, 1)
            v.wait_ge(s_init, 3)
            st.made(v.tensor_tensor(lbt[:, 2, :], lbt[:, 0, :], lbt[:, 1, :], ALU.add))
            st.settle()
            st.made(v.reciprocal(lbt[:, 2, :], lbt[:, 2, :]))
            st.settle()
            st.made(v.tensor_tensor(lbt[:, 0, :], lbt[:, 0, :], lbt[:, 2, :], ALU.mult))
            st.made(v.tensor_tensor(lbt[:, 1, :], lbt[:, 1, :], lbt[:, 2, :], ALU.mult))
            st.settle()
            st.made(v.tensor_tensor(lb[:, 0, :], lbt[:, 0, :], lbt[:, 0, :], ALU.subtract))
            st.made(v.tensor_tensor(lbt[:, 1, :], lbt[:, 0, :], lbt[:, 1, :], ALU.add))
            st.settle()
            st.made(v.tensor_tensor(lb[:, 1, :], lbt[:, 1, :], lbt[:, 0, :], ALU.subtract))
            st.settle()
            v.tensor_scalar(rest[:, :, :], lb[:, :, :], -1.0, 1.0, ALU.mult, ALU.add).then_inc(s_initd, 1)
            st.made(v.tensor_tensor(neglam[:, :], lams[:, :, 1], lams[:, :, 0], ALU.subtract))
            st.settle()
            st.made(v.tensor_tensor(neglam[:, :], neglam[:, :], lam_init[:, :, 0], ALU.subtract))
            for l in range(DEPTH):
                st.made(v.tensor_scalar(gain_da[:, l, :], gain_da[:, l, :], lam_init[:, l, 1:2], None, ALU.mult))
            st.made(v.tensor_copy(lams[:, :, 0], lams[:, :, 1]))
            st.settle()
            st.end()
            v.memset(lbt[:, 2, 0:1], 0.0).then_inc(s_initd, 2)
            v.wait_ge(s_initd, 5)

            hg = Steps(v, h_v, 37)
            das, fxs = Steps(v, da.v, 5 * T + 5), Steps(v, fx.v, 2 * T + 2)
            fs = Steps(v, f_v, 2)
            rs = Steps(v, r_v, 50)
            ms = Steps(v, m_v, 3)
            cs = Steps(v, c_v, T)

            def squares(st, x, sq, ready, turn):
                st.settle()
                st.made(v.tensor_tensor(sq, x, x, ALU.mult))
                st.settle()
                v.tensor_reduce(ss[:, :], sq, AX.X, ALU.add).then_inc(ready, 1)
                st.after(ready, turn + 1)

            def attend_dve(a, st, layer, head, turn):
                U, maps = a.U, a.maps
                groups = sum(len(groups_of(j)) for j in range(T))
                A0, G0, V0 = turn * U, turn * groups * maps, turn * 6 * maps
                st.begin(turn)
                if a is da:
                    v.wait_ge(a.raw, ONE + turn + 1)
                    v.wait_ge(a.perm, ONE + turn + 1)
                    st.made(v.tensor_tensor(rot, bigps[1][:, 0:L], sin, ALU.mult))
                    st.made(v.tensor_tensor(raw, raw, cos, ALU.mult))
                    st.settle()
                    st.made(v.tensor_tensor(qT[0:AW], raw[0:AW], rot[0:AW], ALU.add))
                    v.tensor_tensor(kT[0:AW], raw[AW:2 * AW], rot[AW:2 * AW], ALU.add).then_inc(a.qk, 1)
                    st.after(a.qk, turn + 1)
                else:
                    v.wait_ge(a.proj, ONE + turn + 1)
                    v.wait_ge(a.S, ONE + A0)
                    v.tensor_scalar(qT[0:AW], bigps[0][0:AW, 0:L], AW ** -0.5, None, ALU.mult).then_inc(a.qd, 1)
                    st.after(a.qd, turn + 1)

                def maxima(u):
                    c, j = divmod(u, T)
                    r, n = rows(j), META + P * j
                    S_ = bigps[j % 2]
                    v.wait_ge(a.S, ONE + A0 + u + 1)
                    st.made(v.tensor_tensor(S_[0:r, cols(j)], S_[0:r, cols(j)], causal[0:r, 0:r], ALU.add))
                    st.settle()
                    v.tensor_reduce(negmax[0:r, u:u + 1], S_[0:r, 0:n], AX.X, ALU.max, negate=True)\
                     .then_inc(a.max, 1)
                    st.after(a.max, A0 + u + 1)

                turned = others = 0
                maxima(0)
                for u in range(U):
                    c, j = divmod(u, T)
                    r = rows(j)
                    if u + 1 < U:
                        maxima(u + 1)
                    for gi, g in enumerate(groups_of(j)):
                        turned += 1
                        if gi == 0:
                            continue
                        others += 1
                        v.wait_ge(a.TP, ONE + G0 + turned)
                        v.wait_ge(a.pv, ONE + A0 + max(u - 1, 0))
                        v.tensor_copy(PT[:, u % 2, g[0]:g[-1] + 1, :],
                                      ps[:, 6 + (turned - 1) % 2, 0:len(g) * P].rearrange("p (i n) -> p i n", i=len(g)))\
                         .then_inc(a.ptV, 1)
                        st.after(a.ptV, V0 + others)
                    v.wait_ge(a.P, ONE + A0 + u + 1)
                    st.made(v.reciprocal(rinv[0:r, u:u + 1], rowsum[0:r, u:u + 1]))
                    st.settle()
                    if c == 0:
                        v.wait_ge(a.pv, ONE + A0 + u + 1)
                        v.tensor_scalar(ah[0:r, j, :], ps[0:r, 5, 0:AW], rinv[0:r, u:u + 1], None, ALU.mult)\
                         .then_inc(a.oc, 1)
                    else:
                        st.made(v.tensor_scalar(rneg[0:r, j:j + 1], rinv[0:r, u:u + 1], neglam_l[0:r, :], None,
                                                ALU.mult))
                        st.settle()
                        v.wait_ge(a.pv, ONE + A0 + u + 1)
                        v.scalar_tensor_tensor(out=ah[0:r, j, :], in0=ps[0:r, 5, 0:AW], scalar=rneg[0:r, j:j + 1],
                                               in1=ah[0:r, j, :], op0=ALU.mult, op1=ALU.add).then_inc(a.oc, 1)
                    st.after(a.oc, A0 + u + 1)
                squares(st, ah, asq, a.ss, turn)
                v.wait_ge(a.rstd, ONE + turn + 1)
                gains = gain_da if a is da else gain_fx
                at = 4 * HW if a is da else 4 * HW + HEADS * AW
                st.made(v.tensor_tensor(ah, ah, rstd[:, :].unsqueeze(2).to_broadcast([P, T, AW]), ALU.mult))
                st.settle()
                v.tensor_tensor(mix[:, :, bass.ds(head * AW + at, AW)], ah,
                                gains[:, bass.ds(layer, 1), :].to_broadcast([P, T, AW]), ALU.mult).then_inc(a.out, 1)
                v.wait_ge(a.out, ONE + turn + 1)
                st.end()

            with v.Fori(0, depth) as layer:
                v.wait_ge(s_gamma, layer * 32 + 16)
                for j in range(T + 1):
                    if j < T:
                        norm_apply(0, layer, j)
                    if j >= 1:
                        norm_copy(0, layer, j - 1)
                meet(v, layer, 0)

                if stop > 1:
                    v.memset(ig[:, 0, :], 0.0).then_inc(s_clean, 1)
                    v.memset(AT[:, 0, :], 0.0).then_inc(s_clean, 1)
                    v.wait_ge(s_clean, layer * CLEANS + 2)
                    wait_alone(v, h_const, layer * 32 + 32)
                    with v.Fori(0, HEADS) as head:
                        t = layer * HEADS + head
                        hg.begin(t)
                        lbc = lb[:, bass.ds(layer, 1), bass.ds(head, 1)].rearrange("p a b -> p (a b)")
                        rc = rest[:, bass.ds(layer, 1), bass.ds(head, 1)].rearrange("p a b -> p (a b)")
                        v.wait_ge(h_gexp, ONE + 2 * t + 1)
                        hg.made(v.tensor_scalar(hK, hK, 1.0, None, ALU.add))
                        hg.settle()
                        hg.made(v.reciprocal(hK, hK))
                        hg.settle()
                        hg.made(v.tensor_scalar(hX[0], hK, rc, lbc, ALU.mult, ALU.add))
                        hg.settle()
                        hg.made(v.tensor_scalar(hk, hX[0], -1.0, 1.0, ALU.mult, ALU.add))
                        hg.settle()
                        v.tensor_scalar(hX[0], hX[0], TINY, None, ALU.max).then_inc(h_clamped, 1)
                        v.wait_ge(h_gexp, ONE + 2 * t + 2)
                        hg.made(v.tensor_scalar(hQ, hQ, 1.0, None, ALU.add))
                        hg.settle()
                        hg.made(v.reciprocal(hQ, hQ))
                        hg.settle()
                        hg.made(v.scalar_tensor_tensor(out=hq, in0=bigps[0][:, 0:L], scalar=HW ** -0.5, in1=hQ,
                                                       op0=ALU.mult, op1=ALU.mult))
                        v.wait_ge(h_logf, ONE + t + 1)
                        v.tensor_tensor_scan(hG, reset, hX[1], 0.0, ALU.mult, ALU.add).then_inc(h_diff, 1)
                        hg.after(h_diff, t * 9 + 1)

                        def halves(x, li, part):
                            n = LEVELS[li]
                            lo = 0 if n < META else META
                            return x[:, lo:L].rearrange("p (b s n) -> p b s n", s=2, n=n)[:, :, part, :]

                        def differences(i):
                            X = hX[i % 2]
                            hg.settle()
                            if i <= 7:
                                li = i - 1
                                n = LEVELS[li]
                                ref = halves(hG, li, 0)[:, :, n - 1:n]
                                nb = ref.shape[1]
                                hg.made(v.tensor_tensor(halves(X, li, 0), ref.to_broadcast([P, nb, n]),
                                                        halves(hG, li, 0), ALU.subtract))
                                v.tensor_tensor(halves(X, li, 1), halves(hG, li, 1), ref.to_broadcast([P, nb, n]),
                                                ALU.subtract).then_inc(h_diff, 1)
                            else:
                                hg.made(v.tensor_tensor(X[:, 0:META], hG[:, META - 1:META].to_broadcast([P, META]),
                                                        hG[:, 0:META], ALU.subtract))
                                g3 = hG[:, META:L].rearrange("p (b n) -> p b n", n=P)
                                v.tensor_tensor(X[:, META:L].rearrange("p (b n) -> p b n", n=P),
                                                g3[:, :, P - 1:P].to_broadcast([P, T - 1, P]), g3,
                                                ALU.subtract).then_inc(h_diff, 1)
                            hg.after(h_diff, t * 9 + i + 1)

                        def factors(i):
                            X = hX[i % 2]
                            v.wait_ge(h_decay, ONE + t * 9 + i + 1)
                            if i == 0:
                                v.tensor_tensor(hQ, hq, X, ALU.mult).then_inc(h_factor, 1)
                            elif i <= 7:
                                li = i - 1
                                hg.made(v.tensor_tensor(halves(QK[:, li, :], li, 0), halves(hk, li, 0),
                                                        halves(X, li, 0), ALU.mult))
                                v.tensor_tensor(halves(QK[:, li, :], li, 1), halves(hq, li, 1),
                                                halves(X, li, 1), ALU.mult).then_inc(h_factor, 1)
                            else:
                                v.tensor_tensor(hK, hk, X, ALU.mult).then_inc(h_factor, 1)
                            hg.after(h_factor, t * 9 + i + 1)

                        for i in range(1, 10):
                            if i <= 8:
                                differences(i)
                            factors(i - 1)

                        def within(j):
                            r = rows(j)
                            v.wait_ge(h_lvl, ONE + t * T + j + 1)
                            lo = 0 if j else sum(n >= META for n in LEVELS)
                            A_ = bigps[j % 2][0:r, 0:NL * P].rearrange("p (l n) -> p l n", l=NL)[:, lo:NL, 0:r]
                            hg.made(v.tensor_tensor(A_, A_, masks[0:r, lo:NL, 0:r], ALU.mult))
                            hg.settle()
                            v.wait_ge(h_o, ONE + t * T + max(j - 1, 0))
                            v.tensor_reduce(AT[0:r, j % 2, 0:r], A_.rearrange("p l n -> p n l"), AX.X, ALU.add)\
                             .then_inc(h_at, 1)
                            hg.after(h_at, t * T + j + 1)

                        within(0)
                        v.wait_ge(h_glast, ONE + t + 1)
                        for j in range(T):
                            if j + 1 < T:
                                within(j + 1)
                            if j < T - 1:
                                v.wait_ge(h_ds, ONE + t * (T - 1) + j + 1)
                                if j == 0:
                                    v.tensor_copy(S[:, 0, :], ps[:, 7, 0:HW]).then_inc(h_S, 1)
                                else:
                                    v.wait_ge(h_S, ONE + t * (T - 1) + j)
                                    v.scalar_tensor_tensor(out=S[:, j % 2, :], in0=S[:, (j - 1) % 2, :],
                                                           scalar=glast[:, j:j + 1], in1=ps[:, 7, 0:HW],
                                                           op0=ALU.mult, op1=ALU.add).then_inc(h_S, 1)
                                hg.after(h_S, t * (T - 1) + j + 1)
                        v.wait_ge(h_oc, ONE + t * T + T)
                        squares(hg, oh, osq, h_ss, t)
                        v.wait_ge(h_eg, ONE + t + 1)
                        hg.made(v.tensor_scalar(eg, eg, 1.0, None, ALU.add))
                        hg.settle()
                        hg.made(v.reciprocal(eg, eg))
                        hg.settle()
                        hg.made(v.tensor_tensor(eg, eg, ig[:, :, HW:2 * HW], ALU.mult))
                        v.wait_ge(h_rstd, ONE + t + 1)
                        hg.made(v.tensor_tensor(oh, oh, rstd[:, :].unsqueeze(2).to_broadcast([P, T, HW]), ALU.mult))
                        hg.settle()
                        hg.made(v.tensor_tensor(oh, oh, gain_hg[:, bass.ds(layer, 1), :].to_broadcast([P, T, HW]),
                                                ALU.mult))
                        hg.settle()
                        v.tensor_tensor(mix[:, :, bass.ds(head * HW, HW)], oh, eg, ALU.mult).then_inc(h_out, 1)
                        v.wait_ge(h_out, ONE + t + 1)
                        hg.end()
                    meet(v, layer, 1)

                if stop > 2:
                    v.memset(PT[:, :, 0, :], 0.0).then_inc(s_clean, 1)
                    v.memset(Pr[:, :, 0:P], 0.0).then_inc(s_clean, 1)
                    v.memset(V[:, 0, :], 0.0).then_inc(s_clean, 1)
                    v.memset(ah[:, 0, :], 0.0).then_inc(s_clean, 1)
                    v.tensor_copy(neglam_l[:, :], neglam[:, bass.ds(layer, 1)]).then_inc(s_clean, 1)
                    v.wait_ge(s_clean, layer * CLEANS + 7)
                    wait_alone(v, v_w, layer * 64 + 64)
                    with v.Fori(0, HEADS) as head:
                        attend_dve(da, das, layer, head, layer * HEADS + head)
                    meet(v, layer, 2)

                if stop > 3:
                    fs.begin(layer)
                    v.memset(qT[AW:AW + 2], 1.0).then_inc(s_clean, 1)
                    v.memset(kT[AW:AW + 2], 1.0).then_inc(s_clean, 1)
                    v.wait_ge(s_clean, layer * CLEANS + 9)
                    v.wait_ge(f_p, ONE + layer + 1)
                    v.tensor_scalar(raw[0:HEADS], bigps[0][0:HEADS, 0:L], fbias[:, bass.ds(layer, 1)], None, ALU.add)\
                     .then_inc(f_x, 1)
                    v.wait_ge(f_x, ONE + layer + 1)
                    fs.made(v.tensor_scalar(rot[0:HEADS], raw[0:HEADS], -1.0, 0.0, ALU.mult, ALU.max))
                    fs.settle()
                    v.wait_ge(f_l, ONE + layer + 1)
                    fs.made(v.tensor_tensor(rot[0:HEADS], rot[0:HEADS], Pr[0:HEADS, 0, :], ALU.add))
                    fs.settle()
                    v.tensor_tensor_scan(raw[0:HEADS], rot[0:HEADS], rot[0:HEADS], 0.0, ALU.add, ALU.max)\
                     .then_inc(f_d, 1)
                    v.wait_ge(f_d, ONE + layer * 2 + 1)
                    v.tensor_scalar(rot[0:HEADS], raw[0:HEADS], -1.0, None, ALU.mult).then_inc(f_d, 1)
                    fs.end()
                    with v.Fori(0, HEADS) as head:
                        attend_dve(fx, fxs, layer, head, layer * HEADS + head)
                    meet(v, layer, 3)

                if stop > 4:
                    def copy_mT(j):
                        v.wait_ge(p_tp, ONE + layer * 2 * T + 2 * j + 2)
                        v.wait_ge(p_mm, ONE + layer * T + max(j - 1, 0))
                        v.tensor_copy(mT[:, j % 2, 4:8, 0:rows(j)],
                                      ps[:, 7, :].rearrange("p (k n) -> p k n", k=4)[:, :, 0:rows(j)])\
                         .then_inc(p_tv, 1)

                    copy_mT(0)
                    for j in range(T):
                        r = rows(j)
                        if j + 1 < T:
                            copy_mT(j + 1)
                        v.wait_ge(p_mm, ONE + layer * T + j + 1)
                        v.tensor_tensor(h[0:r, j, :], h[0:r, j, :], bigps[j % 2][0:r, 0:D], ALU.add)\
                         .then_inc(p_h, 1)
                        norm_apply(1, layer, j)
                        if j >= 1:
                            norm_copy(1, layer, j - 1)
                    norm_copy(1, layer, T - 1)
                    meet(v, layer, 4)

                if stop > 5:
                    rs.begin(layer)

                    def do(ins):
                        rs.made(ins)
                        rs.settle()

                    def first_max(x, m, order, t_, o_, n):
                        do(v.tensor_reduce(m, x, AX.X, ALU.max))
                        do(v.tensor_tensor(t_, x, m.unsqueeze(2).to_broadcast([P, T, n]), ALU.is_ge))
                        do(v.tensor_tensor(t_, t_, order.unsqueeze(1).to_broadcast([P, T, n]), ALU.mult))
                        do(v.tensor_reduce(tm, t_, AX.X, ALU.max))
                        do(v.tensor_tensor(o_, t_, tm.unsqueeze(2).to_broadcast([P, T, n]), ALU.is_ge))

                    do(v.memset(ones, 1.0))
                    do(v.memset(lg, 0.0))
                    v.wait_ge(r_w, layer * 112 + 112)
                    v.wait_ge(r_lg, ONE + layer + 1)
                    pl = ps[:, 0, 0:T * ROUTES].rearrange("p (j e) -> p j e", j=T)
                    do(v.tensor_tensor(lg[0:META, 0, :], pl[0:META, 0, :], b_r[0:META, :], ALU.add))
                    do(v.tensor_tensor(lg[:, 1:T, :], pl[:, 1:T, :],
                                       b_r.unsqueeze(1).to_broadcast([P, T - 1, ROUTES]), ALU.add))
                    first_max(lg[:, :, 0:GROUPS], gm, first4, g4, ohg, GROUPS)
                    v.tensor_tensor(g4, lg[:, :, 0:GROUPS], gm.unsqueeze(2).to_broadcast([P, T, GROUPS]),
                                    ALU.subtract).then_inc(r_m, 1)
                    v.wait_ge(r_exp, ONE + layer * 2 + 1)
                    do(v.tensor_reduce(psel, g4, AX.X, ALU.add))
                    do(v.reciprocal(psel, psel))
                    e4 = lg[:, :, GROUPS:ROUTES].rearrange("p j (g e) -> p j g e", g=GROUPS)
                    b4 = big.rearrange("p j (g e) -> p j g e", g=GROUPS)
                    do(v.tensor_tensor(b4, e4, ohg.unsqueeze(3).to_broadcast([P, T, GROUPS, PER_GROUP]), ALU.mult))
                    do(v.tensor_reduce(ein, b4.rearrange("p j g e -> p j e g"), AX.X, ALU.add))
                    first_max(ein, m1, first8, t8, o1, PER_GROUP)
                    do(v.scalar_tensor_tensor(out=ein, in0=o1, scalar=NEG, in1=ein, op0=ALU.mult, op1=ALU.add))
                    first_max(ein, m2, first8, t8, o2, PER_GROUP)
                    v.tensor_tensor(tm, m2, m1, ALU.subtract).then_inc(r_m, 1)
                    v.wait_ge(r_exp, ONE + layer * 2 + 2)
                    do(v.tensor_scalar(m1, tm, 1.0, None, ALU.add))
                    do(v.reciprocal(m1, m1))
                    do(v.tensor_tensor(gate[:, 0, :], m1, psel, ALU.mult))
                    do(v.tensor_tensor(gate[:, 1, :], gate[:, 0, :], tm, ALU.mult))
                    do(v.tensor_tensor(ohg, ohg, valid.unsqueeze(2).to_broadcast([P, T, GROUPS]), ALU.mult))
                    for k, o in ((0, o1), (1, o2)):
                        do(v.tensor_tensor(E[k].rearrange("p j (g e) -> p j g e", g=GROUPS),
                                           ohg.unsqueeze(3).to_broadcast([P, T, GROUPS, PER_GROUP]),
                                           o.unsqueeze(2).to_broadcast([P, T, GROUPS, PER_GROUP]), ALU.mult))
                    v.tensor_tensor(both, E[0], E[1], ALU.add).then_inc(r_A, 1)
                    v.wait_ge(r_A, ONE + layer + 1)
                    v.tensor_reduce(tot, both.rearrange("p j e -> p e j"), AX.X, ALU.add).then_inc(r_tot, 1)
                    v.wait_ge(r_cnt, ONE + layer + 1)
                    do(v.tensor_scalar(cnt_i, ps[:, 2, 0:EXPERTS], float(P - 1), None, ALU.add))
                    do(v.tensor_scalar(cnt_i, cnt_i, 7, None, ALU.arith_shift_right))
                    do(v.tensor_copy(nblk, cnt_i))
                    do(v.tensor_tensor_scan(upto, nblk, nblk, 0.0, ALU.add, ALU.max))
                    do(v.tensor_tensor(base, upto, nblk, ALU.subtract))
                    do(v.tensor_scalar(base, base, float(P), None, ALU.mult))
                    v.wait_ge(r_rank, ONE + layer + 1)
                    do(v.tensor_tensor(place, ps[:, 1, 0:T * EXPERTS].rearrange("p (j e) -> p j e", j=T),
                                       base.unsqueeze(1).to_broadcast([P, T, EXPERTS]), ALU.add))
                    for k in range(2):
                        do(v.tensor_tensor(E[k], E[k], place, ALU.mult))
                        do(v.tensor_reduce(destf[:, k, :], E[k], AX.X, ALU.add))
                    v.tensor_copy(dest[:, :, :], destf).then_inc(r_dest, 1)
                    do(v.tensor_tensor(cmp[0:1], upto[0:1].unsqueeze(1).to_broadcast([1, BLOCKS, EXPERTS]),
                                       blk_no[0:1].unsqueeze(2).to_broadcast([1, BLOCKS, EXPERTS]), ALU.is_le))
                    do(v.tensor_reduce(blkf[0:1], cmp[0:1], AX.X, ALU.add))
                    do(v.tensor_scalar(blk_expert[:, :], blkf[0:1], float(EXPERTS - 1), None, ALU.min))
                    do(v.tensor_tensor(pairs_f[:, 1:2], pairs_f[:, 0:1], pairs_f[:, 1:2], ALU.add))
                    do(v.tensor_scalar(pairs[:, 0:1], upto[0:1, EXPERTS - 1:EXPERTS], 1.0, None, ALU.add))
                    do(v.tensor_scalar(pairs[:, 0:1], pairs[:, 0:1], 1, None, ALU.arith_shift_right))
                    do(v.tensor_copy(pairs_f[:, 0:1], pairs[:, 0:1]))
                    do(v.tensor_copy(pairs[:, 1:2], pairs_f[:, 1:2]))
                    rs.end()
                    meet(v, layer, 5)

                if stop > 6:
                    before = v.value_load(pairs[0:1, 1:2], min_val=0, max_val=BLOCKS // 2)
                    count = v.value_load(pairs[0:1, 0:1], min_val=1, max_val=BLOCKS // 2)

                    def copy_xt(n):
                        v.wait_ge(m_xt, ONE + n)
                        v.tensor_copy(XT[:, 4:8, :].rearrange("p k n -> p (k n)"), ps[:, 6, :]).then_inc(m_xtc, 1)

                    copy_xt(before * 4 + 2 * layer + 2)
                    with v.Fori(0, count) as i:
                        t = before + i
                        for k in range(2):
                            ms.begin(t * 2 + k)
                            v.wait_ge(m_e, ONE + t * 2 + k + 1)
                            ms.made(v.tensor_scalar(sg, sg, 1.0, None, ALU.add))
                            ms.settle()
                            ms.made(v.reciprocal(sg, sg))
                            ms.settle()
                            ms.made(v.tensor_tensor(sg, ps[:, 0, :], sg, ALU.mult))
                            ms.settle()
                            for q in range(2):
                                if q == 0:
                                    v.wait_ge(m_h, ONE + t * 4 + 2 * k + 2)
                                else:
                                    v.wait_ge(m_up[k], ONE + t + 1)
                                v.wait_ge(m_gt, ONE + t * 4 + 2 * k)
                                f = slice(q * F // 2, (q + 1) * F // 2)
                                v.tensor_tensor(G[:, f], sg[:, f], ps[:, 1 + q, 0:F // 2], ALU.mult).then_inc(m_g, 1)
                            ms.end()
                            copy_xt(t * 4 + 2 * k + 2 * layer + 4)
                            v.wait_ge(m_y[k], ONE + t + 1)
                            v.wait_ge(m_out[k], 16 + t * 16)
                            v.tensor_copy(yb[:, k, 512:1024], ps[:, 4, :]).then_inc(m_yv, 1)
                    meet(v, layer, 6)

                if stop > 7:
                    cs.begin(layer)
                    for j in range(T):
                        r = rows(j)
                        v.wait_ge(c_y[j % 2], (layer * (T // 2 + 1 - j % 2) + j // 2 + 1) * 32)
                        cs.made(v.scalar_tensor_tensor(out=h[0:r, j, :], in0=ya[0:r, j % 2, 0, :],
                                                       scalar=gate[0:r, 0, j:j + 1], in1=h[0:r, j, :],
                                                       op0=ALU.mult, op1=ALU.add))
                        cs.settle()
                        v.scalar_tensor_tensor(out=h[0:r, j, :], in0=ya[0:r, j % 2, 1, :],
                                               scalar=gate[0:r, 1, j:j + 1], in1=h[0:r, j, :],
                                               op0=ALU.mult, op1=ALU.add).then_inc(c_h, 1)
                    cs.end()
                    meet(v, layer, 7)

            if stop >= MEETINGS:
                v.wait_ge(s_gamma, 32 * depth + 16)
                for j in range(1, T):
                    norm_apply(2, 0, j)


def constants():
    f = np.float32
    c = {}
    c["c_ident"] = np.eye(P, dtype=f)
    n = np.arange(P)
    c["c_earlier"] = (n[:, None] < n[None, :]).astype(f)
    c["c_causal"] = np.where(n[None, :] > n[:, None], f(NEG), f(0)).astype(f)
    masks = np.zeros((P, NL, P), f)
    for i, half in enumerate(LEVELS):
        s, t = n[:, None], n[None, :]
        masks[:, i, :] = (s // (2 * half) == t // (2 * half)) & (s % (2 * half) < half) & (t % (2 * half) >= half)
    masks[:, NL - 1, :] = np.eye(P)
    c["c_masks"] = masks
    reset = np.ones((L,), f)
    reset[0] = 0
    reset[META::P] = 0
    c["c_reset"] = reset
    inv = (f(10000.0) ** (-np.arange(0, DQK, 2, dtype=f) / f(DQK))).astype(f)
    ang = np.arange(L, dtype=f)[None, :] * inv[:, None]
    scale = np.where(n < AW, f(DQK) ** f(-0.5), f(1)).astype(f)[:, None]
    c["c_cos"] = (np.cos(ang)[n % (DQK // 2)] * scale).astype(f)
    c["c_sin"] = (np.sin(ang)[n % (DQK // 2)] * scale).astype(f)
    swap = np.zeros((P, P), f)
    for m in range(P):
        if m % DQK < DQK // 2:
            swap[m + DQK // 2, m] = -1
        else:
            swap[m - DQK // 2, m] = 1
    c["c_swap"] = swap
    li = [0.8 - 0.6 * math.exp(-0.3 * l) for l in range(DEPTH)]
    c["c_lam_init"] = np.array([[x, 1.0 - x] for x in li], f)
    valid = np.ones((P, T), f)
    valid[META:, 0] = 0
    c["c_valid"] = valid
    c["c_first4"] = np.tile(np.arange(GROUPS, 0, -1, dtype=f), (P, 1))
    c["c_first8"] = np.tile(np.arange(PER_GROUP, 0, -1, dtype=f), (P, 1))
    c["c_blk_no"] = np.tile(np.arange(BLOCKS, dtype=f), (P, 1))
    return c


def layout(inputs):
    a = {k: np.ascontiguousarray(v) for k, v in inputs.items()}
    hg, at = HEADS * HW, HEADS * AW
    q0, f0, i0, g0 = 0, hg, 2 * hg, 3 * hg
    dq, dk, dv, fq, fk, fv = (4 * hg + i * at for i in range(6))
    ff = 4 * hg + 6 * at
    order = []
    for n in range(HEADS):
        for b in (f0, q0, i0, g0):
            order += list(range(b + n * HW, b + (n + 1) * HW))
    for q, k in ((dq, dk), (fq, fk)):
        for n in range(HEADS):
            for b in (q, k):
                order += list(range(b + n * AW, b + (n + 1) * AW))
    order += list(range(dv, dv + at)) + list(range(fv, fv + at)) + list(range(ff, ff + HEADS))
    a["w_in"] = np.ascontiguousarray(a["w_in"][:, :, order])
    a["w_route"] = np.concatenate([a.pop("w_group"), a.pop("w_router")], axis=2)
    a["b_route"] = np.concatenate([a.pop("b_group"), a.pop("b_router")], axis=1)
    a["hgrn_lb"] = np.ascontiguousarray(a["hgrn_lb"].reshape(DEPTH, HEADS, HW).transpose(2, 0, 1))
    a["fox_bias"] = np.ascontiguousarray(a["fox_bias"].T)
    return a


def kernel(**inputs):
    import concourse.bacc as bacc
    from concourse.bass_utils import run_bass_kernel_spmd

    arrays = layout({k: np.asarray(v) for k, v in inputs.items()})
    arrays.update(constants())
    nc = bacc.Bacc("TRN2", target_bir_lowering=False, num_devices=1)
    args = {k: nc.dram_tensor(k, v.shape, mybir.dt.from_np(v.dtype), kind="ExternalInput").ap()
            for k, v in arrays.items()}
    out = nc.dram_tensor("out", (1, SEQ, D), F32, kind="ExternalOutput").ap()
    build(nc, args, out)
    r = run_bass_kernel_spmd(nc, [arrays], core_ids=[0])
    return r.results[0]["out"]
```

```python
import math
from contextlib import ExitStack

import numpy as np

import concourse.bass as bass
from concourse import mybir

F32 = mybir.dt.float32
I32 = mybir.dt.int32
F32R = mybir.dt.float32r
ALU = mybir.AluOpType
ACT = mybir.ActivationFunctionType
AX = mybir.AxisListType

D = 1024
SEQ = 1024
DEPTH = 2
META = 16
L = META + SEQ
P = 128
T = 1 + SEQ // P
KD = D // P
HEADS = 4
HW = 128
AW = 64
DQK = AW // 2
BAND_DA = HEADS * 4 * HW
BAND_FX = BAND_DA + HEADS * 2 * AW
BAND_V = BAND_FX + HEADS * 2 * AW
BAND_FF = BAND_V + 2 * HEADS * AW
GROUPS = 4
PER_GROUP = 8
EXPERTS = GROUPS * PER_GROUP
ROUTES = GROUPS + EXPERTS
F = D // 2
KF = F // P
EPS = 1e-6
TINY = 1e-30
NEG = -1e30
BLOCKS = (EXPERTS + (2 * L - EXPERTS) // P + 1) // 2 * 2
LEVELS = [64, 32, 16, 8, 4, 2, 1]
NL = len(LEVELS) + 1
PHASES = 8
ONE = 1


def rows(j):
    return META if j == 0 else P


def cols(j):
    return slice(0, META) if j == 0 else slice(META + P * (j - 1), META + P * j)


def chunks(n):
    return [(a, min(a + 512, n)) for a in range(0, n, 512)]


def units_of(half):
    units = [(0, -1, META, True)] if half == 0 else []
    for i in range(T):
        lo = max(0, P * (i - 1) - 512 * half)
        if lo < 512:
            units.append((i, lo, 512 - lo, i > 0 and P * (i - 1) >= 512 * half))
    return units


UNITS = len(units_of(0)) + len(units_of(1))
TILES = [list(range(0, 5)), list(range(5, T))]


class Steps:

    def __init__(self, engine, semaphore, every):
        self.engine, self.semaphore, self.every = engine, semaphore, every

    def begin(self, turn):
        self.turn, self.n = turn, 0
        self.last = (self.semaphore, ONE + turn * self.every)

    def made(self, instruction):
        self.n += 1
        instruction.then_inc(self.semaphore, 1)
        self.last = (self.semaphore, ONE + self.turn * self.every + self.n)

    def after(self, semaphore, value):
        self.last = (semaphore, ONE + value)

    def settle(self):
        self.engine.wait_ge(*self.last)

    def end(self):
        assert self.n == self.every, (self.semaphore, self.n, self.every)


def build(nc, A, out, stop=PHASES, depth=DEPTH):
    nc.disable_value_cache = True
    with ExitStack() as ctx:
        def sb(name, shape, dt=F32):
            return ctx.enter_context(nc.sbuf_tensor(name, shape, dt))

        from_one = []

        def signal(name):
            return ctx.enter_context(nc.semaphore(name))

        def sem(name):
            from_one.append(signal(name))
            return from_one[-1]

        h = sb("h", [P, T, D])
        ident = sb("ident", [P, P])
        causal = sb("causal", [P, P])
        gamma = sb("gamma", [P, D])
        gain_hg = sb("gain_hg", [P, DEPTH, HW])
        gain_da = sb("gain_da", [P, DEPTH, AW])
        gain_fx = sb("gain_fx", [P, DEPTH, AW])
        lb = sb("lb", [P, DEPTH, HEADS])
        rest = sb("rest", [P, DEPTH, HEADS])
        lbt = sb("lbt", [P, 3, HEADS])
        lamv = sb("lamv", [P, DEPTH, 4, DQK])
        lamp = sb("lamp", [P, DEPTH, 2, DQK])
        lams = sb("lams", [P, DEPTH, 2])
        lam_init = sb("lam_init", [P, DEPTH, 2])
        neglam = sb("neglam", [P, DEPTH])
        neglam_l = sb("neglam_l", [P, 1])
        fbias = sb("fbias", [HEADS, DEPTH])
        eps = sb("eps", [P, 1])
        ss = sb("ss", [P, T])
        lnss = sb("lnss", [P, T])
        rstd = sb("rstd", [P, T])
        negmax = sb("negmax", [P, 2 * T])
        rowsum = sb("rowsum", [P, 2 * T])
        rinv = sb("rinv", [P, 2 * T])
        rneg = sb("rneg", [P, T])
        glast = sb("glast", [P, T])
        dest = sb("dest", [P, 2, T], I32)
        gate = sb("gate", [P, 2, T])
        pairs = sb("pairs", [1, 2], I32)
        pairs_f = sb("pairs_f", [1, 2])
        blk_expert = sb("blk_expert", [1, BLOCKS], I32)

        ARENA = 41472
        with nc.sbuf_tensor("arena", [P, ARENA], F32) as arena:
            pass
        SCRATCH = KD * L + T * D
        ROUNDED = 6 * L + 11 * P + 2 * L
        below = sb("below", [P, SCRATCH])
        rounded = sb("rounded", [P, ROUNDED], F32R)
        above = sb("above", [P, ARENA - SCRATCH - ROUNDED])
        uT = arena[:, 0:KD * L].rearrange("p (k n) -> p k n", k=KD)
        mix = arena[:, KD * L:KD * L + T * D].rearrange("p (j d) -> p j d", j=T)

        class Place:
            def __init__(self, at):
                self.at = at

            def take(self, *shape, parts=P):
                n = int(np.prod(shape))
                assert self.at + n <= ARENA - P, (self.at + n, ARENA)
                v = arena[0:parts, self.at:self.at + n]
                self.at += n
                if len(shape) == 2:
                    v = v.rearrange("p (a b) -> p a b", a=shape[0])
                if len(shape) == 3:
                    v = v.rearrange("p (a b c) -> p a b c", a=shape[0], b=shape[1])
                return v

        junk = [arena[:, at:at + D] for at in (SCRATCH + 8 * D, SCRATCH, SCRATCH)]
        zeros = arena[:, ARENA - P:ARENA]

        s = Place(SCRATCH)
        w_fq = s.take(KD, 2 * HW)
        w_ig = s.take(KD, 2 * HW)
        masks = s.take(NL, P)
        reset = s.take(L)
        QK = s.take(len(LEVELS), L)
        hq = s.take(L)
        hk = s.take(L)
        hG = s.take(L)
        hX = [s.take(L), s.take(L)]
        hQ = s.take(L)
        hK = s.take(L)
        ig = s.take(T, 2 * HW)
        AT = s.take(2, P)
        KtT = s.take(2, P)
        S = s.take(2, P)
        x_at = (s.at - 3 * 2 * P - T * 2 * HW) - 4 * L
        oh = arena[:, x_at:x_at + T * HW].rearrange("p (j v) -> p j v", j=T)
        osq = arena[:, x_at - 2 * L:x_at - 2 * L + T * HW].rearrange("p (j v) -> p j v", j=T)
        eg = arena[:, x_at + 2 * L:x_at + 2 * L + T * HW].rearrange("p (j v) -> p j v", j=T)

        s = Place(SCRATCH)
        w_v = s.take(KD, 2 * HEADS * AW)
        s = Place(SCRATCH)
        parts = [rounded[:, i * L:(i + 1) * L] for i in range(4)]
        QP, KP = parts[0:2], parts[2:4]
        xh, xl = rounded[:, 4 * L:5 * L], rounded[:, 5 * L:6 * L]
        DQ, DK = xh, xl
        shift = rounded[:, 6 * L:8 * L].rearrange("p (a n) -> p a n", a=2)
        ones_r, causal_r, ident_r = (rounded[:, 8 * L + i * P:8 * L + (i + 1) * P] for i in range(3))
        sel = rounded[:, 8 * L + 3 * P:8 * L + 11 * P].rearrange("p (a n) -> p a n", a=8)
        s = Place(SCRATCH + ROUNDED)
        w_qk = s.take(KD, 2 * AW)
        w_ff = s.take(KD, HEADS)
        cos = s.take(L)
        sin = s.take(L)
        swap = s.take(P)
        OT = s.take(2, L)
        raw, rot = OT[:, 0, :], OT[:, 1, :]
        PT = s.take(2, 512)
        V = s.take(T, 2 * HEADS * (AW + 1))
        sel_read = PT.rearrange("p a b -> p (a b)").rearrange("p (a b) -> p a b", a=8)
        V4 = V.rearrange("p j (h w) -> p j h w", w=AW + 1)
        Vh = s.take(T, AW + 1)
        O = s.take(2 * T, AW + 1)
        fl = arena[0:HEADS, s.at:s.at + L]
        ah = s.take(T, AW)
        asq = s.take(T, AW)
        decays = cos

        s = Place(0)
        w_o = s.take(KD, D)
        s = Place(SCRATCH + 8 * D)
        uT2 = s.take(KD, L)
        mT = s.take(2, KD, P)

        s = Place(SCRATCH + D)
        w_r = s.take(KD, ROUTES)
        ones = s.take(P)
        earlier = s.take(P)
        b_r = s.take(ROUTES)
        valid = s.take(T)
        first4 = s.take(GROUPS)
        first8 = s.take(PER_GROUP)
        blk_no = s.take(BLOCKS)
        lg = s.take(T, ROUTES)
        gm = s.take(T)
        g4 = s.take(T, GROUPS)
        ohg = s.take(T, GROUPS)
        psel = s.take(T)
        big = s.take(T, EXPERTS)
        ein = s.take(T, PER_GROUP)
        m1 = s.take(T)
        m2 = s.take(T)
        t8 = s.take(T, PER_GROUP)
        o1 = s.take(T, PER_GROUP)
        o2 = s.take(T, PER_GROUP)
        tm = s.take(T)
        E = [s.take(T, EXPERTS), s.take(T, EXPERTS)]
        both = s.take(T, EXPERTS)
        tot = s.take(EXPERTS)
        cnt_i = s.take(EXPERTS).bitcast(I32)
        nblk = s.take(EXPERTS)
        upto = s.take(EXPERTS)
        base = s.take(EXPERTS)
        place = s.take(T, EXPERTS)
        destf = s.take(2, T)
        cmp = s.take(BLOCKS, EXPERTS)
        blkf = s.take(BLOCKS)
        zero32 = s.take(EXPERTS)

        s = Place(0)
        W1, W3, W2 = [s.take(KD, F)], [s.take(KD, F)], []
        s = Place(KD * L)
        xb = s.take(2, D)
        XT = s.take(KD, P)
        sg = s.take(F)
        G = s.take(F)
        GT = s.take(KF, P)
        yb = s.take(2, D)
        assert s.at <= SCRATCH
        s = Place(SCRATCH)
        W2.append(s.take(KF, D))
        W1.append(s.take(KD, F))
        W3.append(s.take(KD, F))
        W2.append(s.take(KF, D))

        s = Place(SCRATCH + 9 * D)
        ya = s.take(2, 2, D)

        ps = ctx.enter_context(nc.psum_tensor("ps", [P, 8, 512], F32))
        flat = ps[:, :, :].rearrange("p b n -> p (b n)")
        bigps = [flat[:, 0:1536], flat[:, 1536:3072]]

        xg = nc.dram_tensor("xg", (BLOCKS * P + P, D), F32, kind="Internal").ap()
        decay_rows = nc.dram_tensor("decay_rows", (2, HEADS, L), F32, kind="Internal").ap()

        met, passed = signal("met"), signal("passed")
        s_start, s_par, s_x0 = signal("s_start"), signal("s_par"), signal("s_x0")
        s_init, s_initd = signal("s_init"), signal("s_initd")
        s_zero, s_zfill = signal("s_zero"), signal("s_zfill")
        s_gamma, s_clean = signal("s_gamma"), signal("s_clean")
        v_init = sem("v_init")
        n_rstd, n_u, n_tp, n_ua, n_uv, n_act = [], [], [], [], [], []
        for which in ("mixn", "ffnn", "last"):
            n_rstd.append(sem(which + "_rstd"))
            n_u.append(sem(which + "_u"))
            n_act.append(sem(which + "_act"))
            if which != "last":
                n_tp.append(sem(which + "_tp"))
                n_ua.append(sem(which + "_ua"))
                n_uv.append(sem(which + "_uv"))
        h_const, h_wfq, h_wig = signal("h_const"), signal("h_wfq"), signal("h_wig")
        h_f, h_q, h_ig, h_igc = sem("h_f"), sem("h_q"), sem("h_ig"), sem("h_igc")
        h_gexp, h_clamped, h_logf, h_diff = sem("h_gexp"), sem("h_clamped"), sem("h_logf"), sem("h_diff")
        h_decay, h_factor, h_glast = sem("h_decay"), sem("h_factor"), sem("h_glast")
        h_lvl, h_at, h_ktT, h_ktTc = sem("h_lvl"), sem("h_at"), sem("h_ktT"), sem("h_ktTc")
        h_o, h_oc, h_ds, h_S = sem("h_o"), sem("h_oc"), sem("h_ds"), sem("h_S")
        h_eg, h_ss, h_rstd, h_out = sem("h_eg"), sem("h_ss"), sem("h_rstd"), sem("h_out")
        h_v, h_a = sem("h_v"), sem("h_a")
        class Attention:
            def __init__(self, kind, maps):
                self.maps, self.U = maps, maps * T
                self.w = signal(f"{kind}_w")
                if maps == 1:
                    self.drow = signal(f"{kind}_drow")
                self.proj, self.qk, self.kc = sem(f"{kind}_proj"), sem(f"{kind}_qk"), sem(f"{kind}_kc")
                self.S, self.max, self.shift = sem(f"{kind}_S"), sem(f"{kind}_max"), sem(f"{kind}_shift")
                self.ST, self.P, self.pv, self.oc = (sem(f"{kind}_ST"), sem(f"{kind}_P"), sem(f"{kind}_pv"),
                                                     sem(f"{kind}_oc"))
                self.ss, self.rstd, self.out = sem(f"{kind}_ss"), sem(f"{kind}_rstd"), sem(f"{kind}_out")
                self.v, self.a = sem(f"{kind}_v"), sem(f"{kind}_a")
                self.tp, self.O, self.vh = sem(f"{kind}_tp"), sem(f"{kind}_O"), sem(f"{kind}_vh")
                if maps == 2:
                    self.raw, self.perm, self.parts, self.rep = (sem(f"{kind}_raw"), sem(f"{kind}_perm"),
                                                                 sem(f"{kind}_parts"), sem(f"{kind}_rep"))

        da, fx = Attention("da", 2), Attention("fx", 1)
        v_w, v_t, v_p, v_c = signal("v_w"), signal("v_t"), sem("v_p"), sem("v_c")
        f_w, f_st = signal("f_w"), signal("f_st")
        f_p, f_x, f_act, f_l, f_d, f_v = (sem(n) for n in ("f_p", "f_x", "f_act", "f_l", "f_d", "f_v"))
        p_w = signal("p_w")
        p_tp, p_ta, p_tv, p_mm, p_h = (sem(n) for n in ("p_tp", "p_ta", "p_tv", "p_mm", "p_h"))
        r_w, r_sc, r_done = signal("r_w"), signal("r_sc"), sem("r_done")
        r_lg, r_v, r_exp, r_m, r_rank, r_cnt, r_dest, r_A, r_tot = (sem(n) for n in (
            "r_lg", "r_v", "r_exp", "r_m", "r_rank", "r_cnt", "r_dest", "r_A", "r_tot"))
        m_x = [signal("m_x0"), signal("m_x1")]
        m_w13 = [signal("m_w13_0"), signal("m_w13_1")]
        m_w2 = [signal("m_w2_0"), signal("m_w2_1")]
        m_xt, m_xtc, m_h, m_e, m_v, m_g, m_gt, m_gtc, m_ya, m_yv = (sem(n) for n in (
            "m_xt", "m_xtc", "m_h", "m_e", "m_v", "m_g", "m_gt", "m_gtc", "m_ya", "m_yv"))
        m_up, m_y = [sem("m_up0"), sem("m_up1")], [sem("m_y0"), sem("m_y1")]
        m_out = [signal("m_out0"), signal("m_out1")]
        c_y = [signal("c_y0"), signal("c_y1")]
        c_h, c_v = sem("c_h"), sem("c_v")
        s_store = signal("s_store")

        block = ctx.enter_context(nc.Block())
        ENG = 5

        def wait_alone(engine, semaphore, value):
            engine.wait_ge(semaphore, value)
            engine.sem_inc(passed, 1)

        def all_met(layer, phase):
            return layer * ((PHASES - 1) * ENG - 1) + (phase + 1) * ENG - 1

        def meet(engine, layer, phase):
            engine.sem_inc(passed, 1)
            engine.drain().then_inc(met, 1)
            wait_alone(engine, met, all_met(layer, phase))

        CLEANS = 12

        def halves_of(a):
            work, first, copies = [], 0, 0
            for c in range(a.maps):
                for half in range(2):
                    copies += 2 - half
                    work.append((c, half, first, copies))
                    first += len(units_of(half))
            return work

        @block.sync
        def _(sp):
            def load_gamma(row):
                sp.dma_start(gamma[:, :], row.partition_broadcast(P)).then_inc(s_gamma, 16)

            sp.dma_start(ident[:, :], A["c_ident"]).then_inc(s_start, 16)
            sp.dma_start(h[0:META, 0, :], A["meta_tokens"]).then_inc(s_x0, 16)
            for j in range(1, T):
                sp.dma_start(h[:, j, :], A["x"][0, P * (j - 1):P * j, :]).then_inc(s_x0, 16)
            for dst, src in (
                (causal[:, :], A["c_causal"]),
                (gain_hg[:, :, :], A["hgrn_norm"].partition_broadcast(P)),
                (gain_da[:, :, :], A["diff_norm"].partition_broadcast(P)),
                (gain_fx[:, :, :], A["fox_norm"].partition_broadcast(P)),
                (lb[:, :, :], A["hgrn_lb"]),
                (lamv[:, :, :, :], A["diff_lambda"].partition_broadcast(P)),
                (lam_init[:, :, :], A["c_lam_init"].partition_broadcast(P)),
                (fbias[:, :], A["fox_bias"]),
            ):
                sp.dma_start(dst, src).then_inc(s_par, 16)

            with sp.Fori(0, depth) as layer:
                load_gamma(A["norm_mix"][layer])
                if stop > 1:
                    w = A["w_in"][layer].rearrange("(p k) c -> p k c", k=KD)
                    sp.dma_start(w_fq, w[:, :, 0:2 * HW]).then_inc(h_wfq, 16)
                    sp.dma_start(w_ig, w[:, :, 2 * HW:4 * HW]).then_inc(h_wig, 16)
                    sp.dma_start(masks, A["c_masks"]).then_inc(h_const, 16)
                    sp.dma_start(reset, A["c_reset"].partition_broadcast(P)).then_inc(h_const, 16)
                meet(sp, layer, 0)
                if stop > 1:
                    load_gamma(A["norm_ffn"][layer])
                    with sp.Fori(1, HEADS) as head:
                        t = layer * HEADS + head
                        w = A["w_in"][layer].rearrange("(p k) c -> p k c", k=KD)
                        wait_alone(sp, h_q, ONE + t)
                        sp.dma_start(w_fq, w[:, :, bass.ds(head * 4 * HW, 2 * HW)]).then_inc(h_wfq, 16)
                        wait_alone(sp, h_ig, ONE + t * T)
                        sp.dma_start(w_ig, w[:, :, bass.ds(head * 4 * HW + 2 * HW, 2 * HW)]).then_inc(h_wig, 16)
                    wait_alone(sp, h_q, ONE + layer * HEADS + HEADS)
                    wait_alone(sp, h_ig, ONE + layer * HEADS * T + HEADS * T)
                    if stop > 2:
                        w = A["w_in"][layer].rearrange("(p k) c -> p k c", k=KD)
                        sp.dma_start(w_v, w[:, :, BAND_V:BAND_FF]).then_inc(v_w, 16)
                    meet(sp, layer, 1)
                if stop > 2:
                    w = A["w_in"][layer].rearrange("(p k) c -> p k c", k=KD)
                    sp.dma_start(w_ff, w[:, :, BAND_FF:BAND_FF + HEADS]).then_inc(f_w, 16)
                    for dst, src in ((cos, "c_cos"), (sin, "c_sin"), (swap, "c_swap"), (sel_read, "c_sel")):
                        sp.dma_start(dst, A[src]).then_inc(v_t, 16)
                    with sp.Fori(0, HEADS) as head:
                        t = layer * HEADS + head
                        w = A["w_in"][layer].rearrange("(p k) c -> p k c", k=KD)
                        wait_alone(sp, da.proj, ONE + t)
                        sp.dma_start(w_qk, w[:, :, bass.ds(head * 2 * AW + BAND_DA, 2 * AW)]).then_inc(da.w, 16)
                    meet(sp, layer, 2)
                if stop > 3:
                    with sp.Fori(0, HEADS) as head:
                        t = layer * HEADS + head
                        w = A["w_in"][layer].rearrange("(p k) c -> p k c", k=KD)
                        wait_alone(sp, fx.proj, ONE + t)
                        sp.dma_start(w_qk, w[:, :, bass.ds(head * 2 * AW + BAND_FX, 2 * AW)]).then_inc(fx.w, 16)
                        wait_alone(sp, s_clean, layer * CLEANS + 12)
                        wait_alone(sp, fx.qk, ONE + t)
                        sp.dma_start(decays[2:4], decay_rows[0:2, bass.ds(head, 1)].rearrange(
                            "a h n -> a (h n)")).then_inc(fx.drow, 16)
                        sp.dma_start(decays[32:34], decay_rows[0:2, bass.ds(head, 1)].rearrange(
                            "a h n -> a (h n)")).then_inc(fx.drow, 16)
                    if stop > 4:
                        wait_alone(sp, fx.proj, ONE + layer * HEADS + HEADS)
                        sp.dma_start(w_o, A["w_out"][layer].rearrange("(k p) c -> p k c", p=P)).then_inc(p_w, 16)
                    meet(sp, layer, 3)
                if stop > 5:
                    sp.dma_start(w_r, A["w_route"][layer].rearrange("(p k) c -> p k c", k=KD)).then_inc(r_w, 16)
                    sp.dma_start(b_r, A["b_route"][layer].partition_broadcast(P)).then_inc(r_w, 16)
                    for dst, src in ((earlier, "c_earlier"), (valid, "c_valid"), (first4, "c_first4"), (first8, "c_first8"),
                                     (blk_no, "c_blk_no")):
                        sp.dma_start(dst, A[src]).then_inc(r_w, 16)
                if stop > 4:
                    meet(sp, layer, 4)
                if stop > 6:
                    wait_alone(sp, r_done, ONE + layer + 1)
                if stop > 5:
                    sp.drain().then_inc(met, 1)
                if stop > 6:
                    before = sp.value_load(pairs[0:1, 1:2], min_val=0, max_val=BLOCKS // 2)
                    count = sp.value_load(pairs[0:1, 0:1], min_val=1, max_val=BLOCKS // 2)
                    with sp.Fori(0, count) as i:
                        t = before + i
                        for k in range(2):
                            e = sp.value_load(blk_expert[0:1, bass.ds(i * 2 + k, 1)], min_val=0,
                                              max_val=EXPERTS - 1)
                            wait_alone(sp, m_up[k], ONE + t)
                            sp.dma_start(W1[k], A["w1"][layer, e].rearrange("(p k) f -> p k f", k=KD))\
                              .then_inc(m_w13[k], 16)
                            sp.dma_start(W3[k], A["w3"][layer, e].rearrange("(p k) f -> p k f", k=KD))\
                              .then_inc(m_w13[k], 16)
                            if k == 0:
                                wait_alone(sp, m_x[0], before * 16 + layer * 16 + 16)
                            wait_alone(sp, m_y[k], ONE + t)
                            sp.dma_start(W2[k], A["w2"][layer, e].rearrange("(j p) d -> p j d", p=P))\
                              .then_inc(m_w2[k], 16)
                    meet(sp, layer, 6)
            if stop >= PHASES:
                load_gamma(A["norm_final"])
                for j in range(1, T):
                    sp.wait_ge(n_u[2], ONE + j)
                    sp.dma_start(out[0, P * (j - 1):P * j, :], mix[:, j, :]).then_inc(s_store, 16)
                sp.wait_ge(s_store, 16 * (T - 1))

        @block.scalar
        def _(act):
            nc.scalar.preload_act_table_set("natural_log_exp_and_others")

            steps = [Steps(act, n_act[0], 2 * T), Steps(act, n_act[1], 2 * T), Steps(act, n_act[2], 2 * (T - 1))]

            def norm_stats(which, turn, j, count=T, first=0):
                r, st = rows(j), steps[which]
                st.made(act.activation(junk[which][0:r], h[0:r, j, :], ACT.Square, accum_out=ss[0:r, j:j + 1]))
                st.settle()
                st.made(act.activation(lnss[0:r, j:j + 1], ss[0:r, j:j + 1], ACT.Ln, bias=eps[0:r, :],
                                       scale=1.0 / D))
                st.settle()
                act.activation(rstd[0:r, j:j + 1], lnss[0:r, j:j + 1], ACT.Exp, scale=-0.5)\
                   .then_inc(n_rstd[which], 1)

            def norm_copy(which, turn, j):
                r = rows(j)
                act.wait_ge(n_tp[which], ONE + turn * 2 * T + 2 * j + 1)
                act.activation((uT, uT2)[which][:, 0:4, cols(j)], ps[:, 2, :].rearrange("p (k n) -> p k n", k=4)[:, :, 0:r],
                               ACT.Copy).then_inc(n_ua[which], 1)

            act.wait_ge(s_initd, 1)
            act.activation(lbt[:, 0, :], lbt[:, 0, :], ACT.Exp).then_inc(s_init, 1)
            act.activation(lbt[:, 1, :], lbt[:, 1, :], ACT.Exp).then_inc(s_init, 1)
            act.wait_ge(s_initd, 2)
            act.activation(lams[:, :, :], lams[:, :, :], ACT.Exp).then_inc(s_init, 1)

            def attend_act(a, layer, head, turn):
                U0 = turn * UNITS * a.maps
                act.wait_ge(a.proj, ONE + turn + 1)
                if a is da:
                    act.activation(raw, bigps[0][:, 0:L], ACT.Copy).then_inc(a.raw, 1)
                    for g in range(2):
                        act.wait_ge(a.rep, ONE + turn * 4 + 2 * g + 1)
                        act.activation(QP[g], bigps[0][:, 0:L], ACT.Copy).then_inc(a.kc, 1)
                else:
                    act.activation(KP[0][AW:2 * AW], bigps[0][AW:2 * AW, 0:L], ACT.Copy).then_inc(a.kc, 1)
                    act.wait_ge(a.kc, ONE + turn * 2 + 1)
                    act.activation(KP[0][0:AW], KP[0].bitcast(F32)[AW:2 * AW], ACT.Copy).then_inc(a.kc, 1)

                def copy_out(c, half, last):
                    act.wait_ge(a.pv, ONE + U0 + last)
                    if half == 0:
                        act.activation(OT[0:AW + 1, c, 0:META], ps[0:AW + 1, 5, 0:META], ACT.Copy).then_inc(a.oc, 1)
                    act.activation(OT[0:AW + 1, c, META + 512 * half:META + 512 * half + 512],
                                   ps[0:AW + 1, 6 + half, :], ACT.Copy).then_inc(a.oc, 1)

                before = None
                for c, half, first, _ in halves_of(a):
                    for n, (i, lo, width, own) in enumerate(units_of(half)):
                        u = first + n
                        act.wait_ge(a.ST, ONE + U0 + u + 1)
                        act.wait_ge(a.pv, ONE + U0 + max(u - 1, 0))
                        act.activation(PT[0:rows(i), u % 2, 0:width], ps[0:rows(i), 3 + u % 2, 0:width],
                                       ACT.Exp).then_inc(a.P, 1)
                        if n == 1 and before is not None:
                            copy_out(*before)
                    before = (c, half, first + len(units_of(half)))
                copy_out(*before)
                act.wait_ge(a.tp, ONE + turn + 1)
                act.activation(O[:, 0:a.U, :].rearrange("p (b s) w -> p b s w", s=6 if a is da else 3),
                               ps[:, 0:3, 0:(6 if a is da else 3) * (AW + 1)].rearrange(
                                   "p b (s w) -> p b s w", w=AW + 1), ACT.Copy).then_inc(a.O, 1)
                head_rstd(a.ss, a.a, a.rstd, turn, AW)

            def head_rstd(ready, own, done, turn, width):
                act.wait_ge(ready, ONE + turn + 1)
                act.activation(lnss[:, :], ss[:, :], ACT.Ln, bias=eps[:, :], scale=1.0 / width).then_inc(own, 1)
                act.wait_ge(own, ONE + turn + 1)
                act.activation(rstd[:, :], lnss[:, :], ACT.Exp, scale=-0.5).then_inc(done, 1)

            with act.Fori(0, depth) as layer:
                act.wait_ge(s_x0, 16 * T)
                act.wait_ge(s_initd, 5)
                steps[0].begin(layer)
                for j in range(T + 1):
                    if j < T:
                        act.wait_ge(c_h, ONE + layer * T + j + 1)
                        norm_stats(0, layer, j)
                    if j >= 1:
                        norm_copy(0, layer, j - 1)
                steps[0].end()
                meet(act, layer, 0)

                if stop > 1:
                    wait_alone(act, s_clean, layer * CLEANS + 2)
                    with act.Fori(0, HEADS) as head:
                        t = layer * HEADS + head

                        def copy_ig(j):
                            r = rows(j)
                            act.wait_ge(h_ig, ONE + t * T + j + 1)
                            if j == 0:
                                act.wait_ge(h_o, ONE + t * T)
                                act.wait_ge(h_ds, ONE + t * (T - 1))
                                act.wait_ge(h_out, ONE + t)
                            act.activation(ig[0:r, j, :], ps[0:r, 6 + j % 2, 0:2 * HW], ACT.Copy).then_inc(h_igc, 1)

                        act.wait_ge(h_f, ONE + t + 1)
                        act.wait_ge(h_out, ONE + t)
                        act.wait_ge(h_ktT, ONE + t * (T - 1))
                        act.activation(hK, bigps[1][:, 0:L], ACT.Exp, scale=-1.0).then_inc(h_gexp, 1)
                        act.wait_ge(h_q, ONE + t + 1)
                        act.wait_ge(h_o, ONE + t * T)
                        act.activation(hQ, bigps[0][:, 0:L], ACT.Exp, scale=-1.0).then_inc(h_gexp, 1)
                        copy_ig(0)
                        act.wait_ge(h_clamped, ONE + t + 1)
                        act.activation(hX[1], hX[0], ACT.Ln).then_inc(h_logf, 1)
                        copy_ig(1)
                        act.wait_ge(h_diff, ONE + t * 9 + 1)
                        act.activation(hX[0], hG, ACT.Exp).then_inc(h_decay, 1)
                        act.activation(glast[:, :], hG[:, META - 1:L:P], ACT.Exp).then_inc(h_glast, 1)
                        copy_ig(2)
                        for i in range(1, 9):
                            act.wait_ge(h_diff, ONE + t * 9 + i + 1)
                            act.activation(hX[i % 2], hX[i % 2], ACT.Exp).then_inc(h_decay, 1)
                            if i + 2 < T:
                                copy_ig(i + 2)
                        for j in range(T):
                            r = rows(j)
                            if j < T - 1:
                                act.wait_ge(h_ktT, ONE + t * (T - 1) + j + 1)
                                act.wait_ge(h_ds, ONE + t * (T - 1) + max(j - 1, 0))
                                act.activation(KtT[0:r, j % 2, :], ps[0:r, 2, 0:P], ACT.Copy).then_inc(h_ktTc, 1)
                            act.wait_ge(h_o, ONE + t * T + j + 1)
                            if j == 0:
                                act.wait_ge(h_factor, ONE + t * 9 + 9)
                            act.activation(oh[0:r, j, :], ps[0:r, 5, 0:HW], ACT.Copy).then_inc(h_oc, 1)
                        act.activation(eg, ig[:, :, HW:2 * HW], ACT.Exp, scale=-1.0).then_inc(h_eg, 1)
                        act.wait_ge(h_eg, ONE + t * 3 + 1)
                        act.activation(eg, eg, ACT.Ln, bias=1.0).then_inc(h_eg, 1)
                        act.wait_ge(h_eg, ONE + t * 3 + 2)
                        act.activation(eg, eg, ACT.Exp, scale=-1.0).then_inc(h_eg, 1)
                        head_rstd(h_ss, h_a, h_rstd, t, HW)
                    meet(act, layer, 1)

                if stop > 2:
                    for j in range(T):
                        act.wait_ge(v_p, ONE + layer * T + j + 1)
                        act.activation(V4[0:rows(j), j, :, 0:AW],
                                       ps[0:rows(j), 3 + j % 2, :].rearrange("p (h w) -> p h w", w=AW),
                                       ACT.Copy).then_inc(v_c, 1)
                    act.wait_ge(f_x, ONE + layer + 1)
                    act.activation(fl, rot[0:HEADS], ACT.Abs).then_inc(f_act, 1)
                    act.wait_ge(f_act, ONE + layer * 2 + 1)
                    act.activation(fl, fl, ACT.Exp, scale=-1.0).then_inc(f_act, 1)
                    act.wait_ge(f_act, ONE + layer * 2 + 2)
                    act.activation(fl, fl, ACT.Ln, bias=1.0).then_inc(f_l, 1)
                    wait_alone(act, f_d, ONE + layer * 4 + 4)
                    with act.Fori(0, HEADS) as head:
                        attend_act(da, layer, head, layer * HEADS + head)
                    meet(act, layer, 2)

                if stop > 3:
                    with act.Fori(0, HEADS) as head:
                        attend_act(fx, layer, head, layer * HEADS + head)
                    meet(act, layer, 3)

                if stop > 4:
                    steps[1].begin(layer)

                    def copy_mT(j):
                        act.wait_ge(p_tp, ONE + layer * 2 * T + 2 * j + 1)
                        act.wait_ge(p_mm, ONE + layer * T + max(j - 1, 0))
                        act.activation(mT[:, j % 2, 0:4, 0:rows(j)],
                                       ps[:, 6, :].rearrange("p (k n) -> p k n", k=4)[:, :, 0:rows(j)],
                                       ACT.Copy).then_inc(p_ta, 1)

                    copy_mT(0)
                    for j in range(T):
                        if j + 1 < T:
                            copy_mT(j + 1)
                        act.wait_ge(p_h, ONE + layer * T + j + 1)
                        norm_stats(1, layer, j)
                        if j >= 1:
                            norm_copy(1, layer, j - 1)
                    norm_copy(1, layer, T - 1)
                    steps[1].end()
                    meet(act, layer, 4)

                if stop > 5:
                    act.wait_ge(r_m, ONE + layer * 2 + 1)
                    act.activation(g4, g4, ACT.Exp).then_inc(r_exp, 1)
                    act.wait_ge(r_m, ONE + layer * 2 + 2)
                    act.activation(tm, tm, ACT.Exp).then_inc(r_exp, 1)
                    meet(act, layer, 5)

                if stop > 6:
                    before = act.value_load(pairs[0:1, 1:2], min_val=0, max_val=BLOCKS // 2)
                    count = act.value_load(pairs[0:1, 0:1], min_val=1, max_val=BLOCKS // 2)
                    act.wait_ge(m_xt, ONE + before * 4 + layer * 2)
                    act.dma_start(xb[:, 0, :], xg[0:P, :]).then_inc(m_x[0], 16)
                    act.wait_ge(m_xt, ONE + before * 4 + layer * 2 + 2)
                    act.activation(XT[:, 0:4, :].rearrange("p k n -> p (k n)"), ps[:, 5, :], ACT.Copy)\
                       .then_inc(m_xtc, 1)
                    with act.Fori(0, count) as i:
                        t = before + i
                        for k in range(2):
                            nxt = 1 - k
                            act.wait_ge(m_xt, ONE + t * 4 + 2 * k + 2 * layer)
                            act.dma_start(xb[:, nxt, :], xg[bass.ds((i * 2 + k + 1) * P, P), :])\
                               .then_inc(m_x[nxt], 16)
                            act.wait_ge(m_h, ONE + t * 4 + 2 * k + 1)
                            act.wait_ge(m_g, ONE + t * 4 + 2 * k)
                            act.activation(sg, ps[:, 0, :], ACT.Exp, scale=-1.0).then_inc(m_e, 1)
                            act.wait_ge(m_xt, ONE + t * 4 + 2 * k + 2 * layer + 4 - 1)
                            act.activation(XT[:, 0:4, :].rearrange("p k n -> p (k n)"), ps[:, 5, :], ACT.Copy)\
                               .then_inc(m_xtc, 1)
                            for q in range(2):
                                act.wait_ge(m_gt, ONE + t * 4 + 2 * k + q + 1)
                                if q == 0:
                                    act.wait_ge(m_y[1 - k], ONE + t + k)
                                act.activation(GT[:, 2 * q:2 * q + 2, :].rearrange("p k n -> p (k n)"),
                                               ps[:, 7, 0:2 * P], ACT.Copy).then_inc(m_gtc, 1)
                            act.wait_ge(m_y[k], ONE + t + 1)
                            act.wait_ge(m_out[k], 16 + t * 16)
                            act.activation(yb[:, k, 0:512], ps[:, 3, :], ACT.Copy).then_inc(m_ya, 1)
                            act.wait_ge(m_ya, ONE + t * 2 + k + 1)
                            act.wait_ge(m_yv, ONE + t * 2 + k + 1)
                            act.dma_start(xg[bass.ds((i * 2 + k) * P, P), :], yb[:, k, :]).then_inc(m_out[k], 16)
                    act.wait_ge(m_out[0], 16 + (before + count) * 16)
                    act.wait_ge(m_out[1], 16 + (before + count) * 16)
                    meet(act, layer, 6)

            if stop >= PHASES:
                steps[2].begin(0)
                for j in range(1, T):
                    act.wait_ge(c_h, ONE + depth * T + j + 1)
                    norm_stats(2, 0, j)
                steps[2].end()

        @block.tensor
        def _(pe):
            def norm_turn(which, turn, j):
                pe.wait_ge(n_u[which], ONE + turn * T + j + 1)
                pe.wait_ge(n_ua[which], ONE + turn * T + j)
                pe.wait_ge(n_uv[which], ONE + turn * T + j)
                for k in range(KD):
                    bank = 2 if k < 4 else 5
                    mm = pe.transpose(ps[:, bank, (k % 4) * P:(k % 4 + 1) * P], mix[:, j, k * P:(k + 1) * P],
                                      ident[:, :])
                    if k % 4 == 3:
                        mm.then_inc(n_tp[which], 1)

            pe.wait_ge(s_start, 16)

            def project(dst, w, lo, hi):
                for a, b in chunks(L):
                    for k in range(KD):
                        mm = pe.matmul(dst[0:hi - lo, a:b], w[:, k, lo:hi], uT[:, k, a:b],
                                       start=(k == 0), stop=(k == KD - 1))
                return mm

            def attend_pe(a, layer, head, turn):
                A0, U0, C0 = turn * a.U, turn * UNITS * a.maps, turn * 3 * a.maps
                pe.wait_ge(a.w, turn * 16 + 16)
                pe.wait_ge(a.max, ONE + A0)
                pe.wait_ge(a.P, ONE + U0)
                pe.wait_ge(a.O, ONE + turn)
                project(bigps[0], w_qk, 0, 2 * AW).then_inc(a.proj, 1)
                if a is da:
                    pe.wait_ge(a.raw, ONE + turn + 1)
                    for x, y in chunks(L):
                        mm = pe.matmul(bigps[1][:, x:y], swap[:, :], raw[:, x:y], start=True, stop=True)
                    mm.then_inc(a.perm, 1)
                    pe.wait_ge(a.parts, ONE + turn + 1)
                    for g in range(4):
                        if g == 2:
                            pe.wait_ge(a.kc, ONE + turn * 2 + 1)
                        if g == 3:
                            pe.wait_ge(a.qk, ONE + turn * 2 + 1)
                        for x, y in chunks(L):
                            pe.matmul(bigps[g % 2][:, x:y], sel[:, 2 * g, :], xh[:, x:y], start=True, stop=False)
                            mm = pe.matmul(bigps[g % 2][:, x:y], sel[:, 2 * g + 1, :], xl[:, x:y],
                                           start=False, stop=True)
                        mm.then_inc(a.rep, 1)
                    pe.wait_ge(a.qk, ONE + turn * 2 + 2)
                else:
                    pe.wait_ge(a.qk, ONE + turn + 1)
                pe.wait_ge(a.kc, ONE + turn * 2 + 2)

                def operands(c):
                    return [(QP[c], KP[c])] if a is da else [(QP[0], KP[0]), (QP[0], KP[1]), (DQ, DK)]

                def scores(u):
                    c, j = divmod(u, T)
                    r, n = rows(j), META + P * j
                    if u >= 1:
                        pe.wait_ge(a.max, ONE + A0 + u)
                    for x, y in chunks(n):
                        for i, (q, k) in enumerate(operands(c)):
                            mm = pe.matmul(bigps[0][0:r, x:y], q[:, cols(j)], k[:, x:y],
                                           start=(i == 0), stop=False, skip_group_check=True)
                        lo = max(x, cols(j).start)
                        if lo < y:
                            at = lo - cols(j).start
                            mm = pe.matmul(bigps[0][0:r, lo:y], ident_r[:, 0:r], causal_r[:, at:at + y - lo],
                                           start=False, stop=True, skip_group_check=True)
                    mm.then_inc(a.S, 1)

                def turned_scores(c, half, u, i, lo, width, own):
                    r = rows(i)
                    keys = slice(cols(i).start, cols(i).start + r)
                    queries = slice(0, META) if lo < 0 else slice(META + 512 * half + lo, META + 512 * half + 512)
                    out = ps[0:r, 3 + u % 2, 0:width]
                    if u >= 2:
                        pe.wait_ge(a.P, ONE + U0 + u - 1)
                    for part in range(2):
                        pe.matmul(out, ones_r[:, 0:r], shift[:, part, queries],
                                  start=(part == 0), stop=False, skip_group_check=True)
                    if own:
                        pe.matmul(ps[0:r, 3 + u % 2, 0:r], causal_r[:, 0:r], ident_r[:, 0:r],
                                  start=False, stop=False, skip_group_check=True)
                    for n, (q, k) in enumerate(operands(c)):
                        mm = pe.matmul(out, k[:, keys], q[:, queries], start=False, stop=(n == len(operands(c)) - 1),
                                       skip_group_check=True)
                    mm.then_inc(a.ST, 1)

                def outputs(c, half, u, i, lo, width, own):
                    r = rows(i)
                    pe.wait_ge(a.P, ONE + U0 + u + 1)
                    out = ps[0:AW + 1, 5, 0:META] if lo < 0 else ps[0:AW + 1, 6 + half, lo:512]
                    pe.matmul(out, Vh[0:r, i, :], PT[0:r, u % 2, 0:width], start=(i == 0),
                              stop=(lo < 0 or width == P), skip_group_check=True).then_inc(a.pv, 1)

                work = halves_of(a)
                todo = []
                for c, half, _, _ in work:
                    todo += [(c, j) for j in TILES[half]]
                done = 0

                def next_scores():
                    nonlocal done
                    scores(todo[done][0] * T + todo[done][1])
                    done += 1

                for _ in TILES[0]:
                    next_scores()
                pe.wait_ge(a.vh, ONE + turn + 1)
                pending = None
                for g, (c, half, first, copies) in enumerate(work):
                    pe.wait_ge(a.shift, ONE + A0 + done)
                    ahead = min(len(TILES[1 - half]), len(todo) - done)
                    for n, unit in enumerate(units_of(half)):
                        turned_scores(c, half, first + n, *unit)
                        if n < ahead:
                            next_scores()
                        if pending is not None:
                            outputs(*pending)
                        if n == 0 and g >= 2:
                            pe.wait_ge(a.oc, ONE + C0 + work[g - 2][3])
                        pending = (c, half, first + n, *unit)
                outputs(*pending)
                pe.wait_ge(a.oc, ONE + C0 + 3 * a.maps)
                per = a.U // 3
                for u in range(a.U):
                    first = cols(u % T).start
                    mm = pe.transpose(ps[:, u // per, (u % per) * (AW + 1):(u % per + 1) * (AW + 1)],
                                      OT[0:AW + 1, u // T, first:first + P], ident[0:AW + 1, 0:AW + 1])
                mm.then_inc(a.tp, 1)

            with pe.Fori(0, depth) as layer:
                for j in range(T):
                    norm_turn(0, layer, j)
                meet(pe, layer, 0)

                if stop > 1:
                    with pe.Fori(0, HEADS) as head:
                        t = layer * HEADS + head
                        pe.wait_ge(h_wfq, t * 16 + 16)
                        pe.wait_ge(h_at, ONE + t * T)
                        pe.wait_ge(h_oc, ONE + t * T)
                        project(bigps[1], w_fq, 0, HW).then_inc(h_f, 1)
                        pe.wait_ge(h_ktTc, ONE + t * (T - 1))
                        project(bigps[0], w_fq, HW, 2 * HW).then_inc(h_q, 1)
                        pe.wait_ge(h_wig, t * 16 + 16)
                        for j in range(T):
                            r = rows(j)
                            pe.wait_ge(h_igc, ONE + t * T + max(j - 1, 0))
                            if j == 1:
                                pe.wait_ge(h_S, ONE + t * (T - 1))
                            for k in range(KD):
                                mm = pe.matmul(ps[0:r, 6 + j % 2, 0:2 * HW], uT[:, k, cols(j)], w_ig[:, k, :],
                                               start=(k == 0), stop=(k == KD - 1))
                            mm.then_inc(h_ig, 1)

                        def levels(j):
                            r = rows(j)
                            if j == 0:
                                pe.wait_ge(h_factor, ONE + t * 9 + 8)
                            pe.wait_ge(h_at, ONE + t * T + max(j - 1, 0))
                            for li in range(NL):
                                if li < NL - 1 and LEVELS[li] >= r:
                                    continue
                                lhs = hk if li == NL - 1 else QK[:, li, :]
                                rhs = hq if li == NL - 1 else QK[:, li, :]
                                mm = pe.matmul(bigps[j % 2][0:r, li * P:li * P + r], lhs[:, cols(j)],
                                               rhs[:, cols(j)], start=True, stop=True)
                            mm.then_inc(h_lvl, 1)

                        levels(0)
                        for j in range(T):
                            r = rows(j)
                            if j + 1 < T:
                                levels(j + 1)
                            if j < T - 1:
                                if j == 0:
                                    pe.wait_ge(h_factor, ONE + t * 9 + 9)
                                pe.wait_ge(h_ktTc, ONE + t * (T - 1) + j)
                                pe.transpose(ps[0:r, 2, 0:P], hK[:, cols(j)], ident[:, :]).then_inc(h_ktT, 1)
                            pe.wait_ge(h_at, ONE + t * T + j + 1)
                            pe.wait_ge(h_igc, ONE + t * T + T)
                            pe.wait_ge(h_oc, ONE + t * T + j)
                            if j > 0:
                                pe.wait_ge(h_S, ONE + t * (T - 1) + j)
                                pe.matmul(ps[0:r, 5, 0:HW], hQ[:, cols(j)], S[:, (j - 1) % 2, :],
                                          start=True, stop=False)
                            pe.matmul(ps[:, 5, 0:HW], AT[0:r, j % 2, :], ig[0:r, j, 0:HW],
                                      start=(j == 0), stop=True).then_inc(h_o, 1)
                            if j < T - 1:
                                pe.wait_ge(h_ktTc, ONE + t * (T - 1) + j + 1)
                                pe.matmul(ps[:, 7, 0:HW], KtT[0:r, j % 2, :], ig[0:r, j, 0:HW],
                                          start=True, stop=True).then_inc(h_ds, 1)
                    meet(pe, layer, 1)

                if stop > 2:
                    pe.wait_ge(v_w, layer * 16 + 16)
                    for j in range(T):
                        pe.wait_ge(v_c, ONE + layer * T + max(j - 1, 0))
                        for k in range(KD):
                            mm = pe.matmul(ps[0:rows(j), 3 + j % 2, :], uT[:, k, cols(j)], w_v[:, k, :],
                                           start=(k == 0), stop=(k == KD - 1))
                        mm.then_inc(v_p, 1)
                    pe.wait_ge(v_c, ONE + layer * T + T)
                    pe.wait_ge(f_w, layer * 16 + 16)
                    project(bigps[0], w_ff, 0, HEADS).then_inc(f_p, 1)
                    wait_alone(pe, f_x, ONE + layer + 1)
                    wait_alone(pe, v_t, layer * 64 + 64)
                    with pe.Fori(0, HEADS) as head:
                        attend_pe(da, layer, head, layer * HEADS + head)
                    meet(pe, layer, 2)

                if stop > 3:
                    with pe.Fori(0, HEADS) as head:
                        attend_pe(fx, layer, head, layer * HEADS + head)
                    meet(pe, layer, 3)

                if stop > 4:
                    def turn_mix(j):
                        r = rows(j)
                        pe.wait_ge(p_ta, ONE + layer * T + j)
                        pe.wait_ge(p_tv, ONE + layer * T + j)
                        for k in range(KD):
                            mm = pe.transpose(ps[:, 6 + k // 4, (k % 4) * P:(k % 4 + 1) * P],
                                              mix[:, j, k * P:(k + 1) * P], ident[:, :])
                            if k % 4 == 3:
                                mm.then_inc(p_tp, 1)

                    turn_mix(0)
                    pe.wait_ge(p_w, layer * 16 + 16)
                    for j in range(T):
                        r = rows(j)
                        if j + 1 < T:
                            turn_mix(j + 1)
                        pe.wait_ge(p_ta, ONE + layer * T + j + 1)
                        pe.wait_ge(p_tv, ONE + layer * T + j + 1)
                        pe.wait_ge(p_h, ONE + layer * T + max(j - 1, 0))
                        for half in range(2):
                            for k in range(KD):
                                mm = pe.matmul(ps[0:r, 3 * (j % 2) + half, :], mT[:, j % 2, k, 0:r],
                                               w_o[:, k, half * 512:half * 512 + 512],
                                               start=(k == 0), stop=(k == KD - 1))
                        mm.then_inc(p_mm, 1)
                        if j >= 1:
                            norm_turn(1, layer, j - 1)
                    norm_turn(1, layer, T - 1)
                    meet(pe, layer, 4)

                if stop > 5:
                    pe.wait_ge(r_w, layer * 112 + 112)
                    for j in range(T):
                        for k in range(KD):
                            mm = pe.matmul(ps[0:rows(j), 0, j * ROUTES:(j + 1) * ROUTES], uT2[:, k, cols(j)],
                                           w_r[:, k, :], start=(k == 0), stop=(k == KD - 1))
                    mm.then_inc(r_lg, 1)
                    pe.wait_ge(r_A, ONE + layer + 1)
                    W = T * EXPERTS
                    pe.matmul(ps[:, 1, 0:W], earlier[:, :], both.rearrange("p j e -> p (j e)"),
                              start=True, stop=False, skip_group_check=True)
                    for j in range(T - 1):
                        for i in range(j + 1, T):
                            mm = pe.matmul(ps[:, 1, i * EXPERTS:(i + 1) * EXPERTS], ones[:, :], both[:, j, :],
                                           start=False, stop=(j == T - 2), skip_group_check=True)
                    mm.then_inc(r_rank, 1)
                    pe.wait_ge(r_tot, ONE + layer + 1)
                    pe.matmul(ps[:, 2, 0:EXPERTS], ones[:, :], tot, start=True, stop=True).then_inc(r_cnt, 1)
                    meet(pe, layer, 5)

                if stop > 6:
                    before = pe.value_load(pairs[0:1, 1:2], min_val=0, max_val=BLOCKS // 2)
                    count = pe.value_load(pairs[0:1, 0:1], min_val=1, max_val=BLOCKS // 2)

                    def turn_rows(k):
                        for c in range(KD):
                            mm = pe.transpose(ps[:, 5 + c // 4, (c % 4) * P:(c % 4 + 1) * P],
                                              xb[:, k, c * P:(c + 1) * P], ident[:, :])
                            if c % 4 == 3:
                                mm.then_inc(m_xt, 1)

                    pe.wait_ge(m_x[0], before * 16 + layer * 16 + 16)
                    turn_rows(0)
                    with pe.Fori(0, count) as i:
                        t = before + i
                        for k in range(2):
                            pe.wait_ge(m_xtc, ONE + t * 4 + 2 * k + 2 * layer + 2)
                            pe.wait_ge(m_w13[k], t * 32 + 32)
                            pe.wait_ge(m_g, ONE + t * 4 + 2 * k)
                            for c in range(KD):
                                mm = pe.matmul(ps[:, 0, :], XT[:, c, :], W1[k][:, c, :],
                                               start=(c == 0), stop=(c == KD - 1))
                            mm.then_inc(m_h, 1)
                            for q in range(2):
                                for c in range(KD):
                                    mm = pe.matmul(ps[:, 1 + q, 0:F // 2], XT[:, c, :],
                                                   W3[k][:, c, q * F // 2:(q + 1) * F // 2],
                                                   start=(c == 0), stop=(c == KD - 1))
                                mm.then_inc(m_h if q == 0 else m_up[k], 1)
                            if k == 0:
                                pe.wait_ge(m_x[1], t * 16 + 16)
                            else:
                                pe.wait_ge(m_x[0], t * 16 + layer * 16 + 32)
                            turn_rows(1 - k)
                            pe.wait_ge(m_w2[k], t * 16 + 16)
                            pe.wait_ge(m_ya, ONE + t * 2 + k)
                            pe.wait_ge(m_yv, ONE + t * 2 + k)
                            for q in range(2):
                                pe.wait_ge(m_g, ONE + t * 4 + 2 * k + q + 1)
                                pe.wait_ge(m_gtc, ONE + t * 4 + 2 * k + q)
                                for c in range(2):
                                    f0 = (2 * q + c) * P
                                    mm = pe.transpose(ps[:, 7, c * P:(c + 1) * P], G[:, f0:f0 + P], ident[:, :])
                                mm.then_inc(m_gt, 1)
                                pe.wait_ge(m_gtc, ONE + t * 4 + 2 * k + q + 1)
                                for half in range(2):
                                    for c in range(2 * q, 2 * q + 2):
                                        mm = pe.matmul(ps[:, 3 + half, :], GT[:, c, :],
                                                       W2[k][:, c, half * 512:half * 512 + 512],
                                                       start=(c == 0), stop=(c == KF - 1))
                            mm.then_inc(m_y[k], 1)
                    meet(pe, layer, 6)

        @block.gpsimd
        def _(pool):
            for semaphore in from_one:
                pool.sem_inc(semaphore, ONE)
            pool.sem_inc(c_h, T)
            for semaphore in m_out:
                pool.sem_inc(semaphore, 16)
            wait_alone(pool, s_zero, 1)
            wait_alone(pool, h_wfq, 16)
            wait_alone(pool, h_wig, 16)
            wait_alone(pool, s_par, 16 * 8)
            for b in range(BLOCKS + 1):
                pool.dma_start(xg[b * P:(b + 1) * P, :].rearrange("p (a n) -> p a n", n=P),
                               zeros.unsqueeze(1).to_broadcast([P, D // P, P])).then_inc(s_zfill, 16)
            with pool.Fori(0, depth) as layer:
                wait_alone(pool, met, all_met(layer, 0))
                for phase in range(1, min(5, stop)):
                    if phase == 2:
                        wait_alone(pool, f_d, ONE + layer * 4 + 4)
                        pool.dma_start(decay_rows[0], xh.bitcast(F32)[0:HEADS]).then_inc(f_st, 16)
                        pool.dma_start(decay_rows[1], xl.bitcast(F32)[0:HEADS]).then_inc(f_st, 16)
                        wait_alone(pool, f_st, layer * 32 + 32)
                    meet(pool, layer, phase)
                if stop > 5:
                    wait_alone(pool, s_zfill, 16 * (BLOCKS + 1))
                    wait_alone(pool, r_dest, ONE + layer + 1)
                    for k in range(2):
                        for j in range(T):
                            pool.indirect_dma_start(
                                out=xg[:, :], out_offset=bass.IndirectOffsetOnAxis(ap=dest[0:rows(j), k, j:j + 1], axis=0),
                                in_=mix[0:rows(j), j, :], in_offset=None).then_inc(r_sc, 16)
                    wait_alone(pool, r_sc, layer * 32 * T + 32 * T)
                    meet(pool, layer, 5)
                if stop > 6:
                    meet(pool, layer, 6)
                if stop > 7:
                    for j in range(T):
                        wait_alone(pool, c_h, ONE + T + layer * T + max(j - 1, 0))
                        for k in range(2):
                            pool.indirect_dma_start(
                                out=ya[0:rows(j), j % 2, k, :], out_offset=None, in_=xg[:, :],
                                in_offset=bass.IndirectOffsetOnAxis(ap=dest[0:rows(j), k, j:j + 1], axis=0))\
                                .then_inc(c_y[j % 2], 16)

        @block.vector
        def _(v):
            def norm_apply(which, turn, j, count=T):
                r = rows(j)
                v.wait_ge(n_rstd[which], ONE + turn * T + j + (1 if which < 2 else 0))
                perm = "p (n k) -> p k n"
                v.scalar_tensor_tensor(
                    out=mix[0:r, j, :].rearrange("p (k n) -> p k n", k=KD) if which < 2 else mix[0:r, j, :],
                    in0=h[0:r, j, :].rearrange(perm, k=KD) if which < 2 else h[0:r, j, :],
                    scalar=rstd[0:r, j:j + 1],
                    in1=gamma[0:r, :].rearrange(perm, k=KD) if which < 2 else gamma[0:r, :],
                    op0=ALU.mult, op1=ALU.mult).then_inc(n_u[which], 1)

            def norm_copy(which, turn, j):
                v.wait_ge(n_tp[which], ONE + turn * 2 * T + 2 * j + 2)
                v.tensor_copy((uT, uT2)[which][:, 4:8, cols(j)], ps[:, 5, :].rearrange("p (k n) -> p k n", k=4)[:, :, 0:rows(j)])\
                 .then_inc(n_uv[which], 1)

            v.memset(zeros, 0.0).then_inc(s_zero, 1)
            v.memset(eps[:, :], EPS)
            v.memset(pairs_f[:, :], 0.0)
            v.memset(arena[:, KD * L:KD * L + D], 0.0)
            v.memset(ss[:, :], 1.0)
            v.memset(negmax[:, :], 0.0)
            v.memset(rowsum[:, :], 1.0)
            v.memset(flat[:, 3072:4096], 0.0)
            st = Steps(v, v_init, 15)
            st.begin(0)
            v.wait_ge(s_par, 16 * 8)
            st.made(v.tensor_tensor(lbt[:, 2, :], lb[:, 0, :], lb[:, 1, :], ALU.max))
            st.settle()
            st.made(v.tensor_tensor(lbt[:, 0, :], lb[:, 0, :], lbt[:, 2, :], ALU.subtract))
            v.tensor_tensor(lbt[:, 1, :], lb[:, 1, :], lbt[:, 2, :], ALU.subtract).then_inc(s_initd, 1)
            st.made(v.tensor_tensor(lamp[:, :, :, :], lamv[:, :, 0:4:2, :], lamv[:, :, 1:4:2, :], ALU.mult))
            st.settle()
            v.tensor_reduce(lams[:, :, :], lamp[:, :, :, :], AX.X, ALU.add).then_inc(s_initd, 1)
            v.wait_ge(s_init, 3)
            st.made(v.tensor_tensor(lbt[:, 2, :], lbt[:, 0, :], lbt[:, 1, :], ALU.add))
            st.settle()
            st.made(v.reciprocal(lbt[:, 2, :], lbt[:, 2, :]))
            st.settle()
            st.made(v.tensor_tensor(lbt[:, 0, :], lbt[:, 0, :], lbt[:, 2, :], ALU.mult))
            st.made(v.tensor_tensor(lbt[:, 1, :], lbt[:, 1, :], lbt[:, 2, :], ALU.mult))
            st.settle()
            st.made(v.tensor_tensor(lb[:, 0, :], lbt[:, 0, :], lbt[:, 0, :], ALU.subtract))
            st.made(v.tensor_tensor(lbt[:, 1, :], lbt[:, 0, :], lbt[:, 1, :], ALU.add))
            st.settle()
            st.made(v.tensor_tensor(lb[:, 1, :], lbt[:, 1, :], lbt[:, 0, :], ALU.subtract))
            st.settle()
            v.tensor_scalar(rest[:, :, :], lb[:, :, :], -1.0, 1.0, ALU.mult, ALU.add).then_inc(s_initd, 1)
            st.made(v.tensor_tensor(neglam[:, :], lams[:, :, 1], lams[:, :, 0], ALU.subtract))
            st.settle()
            st.made(v.tensor_tensor(neglam[:, :], neglam[:, :], lam_init[:, :, 0], ALU.subtract))
            for l in range(DEPTH):
                st.made(v.tensor_scalar(gain_da[:, l, :], gain_da[:, l, :], lam_init[:, l, 1:2], None, ALU.mult))
            st.made(v.tensor_copy(lams[:, :, 0], lams[:, :, 1]))
            st.settle()
            st.end()
            v.memset(lbt[:, 2, 0:1], 0.0).then_inc(s_initd, 2)
            v.wait_ge(s_initd, 5)

            hg = Steps(v, h_v, 35)
            das, fxs = Steps(v, da.v, 2 * T + 11), Steps(v, fx.v, T + 9)
            fs = Steps(v, f_v, 1)
            rs = Steps(v, r_v, 49)
            ms = Steps(v, m_v, 3)
            cs = Steps(v, c_v, T)

            def squares(st, x, sq, ready, turn):
                st.settle()
                st.made(v.tensor_tensor(sq, x, x, ALU.mult))
                st.settle()
                v.tensor_reduce(ss[:, :], sq, AX.X, ALU.add).then_inc(ready, 1)
                st.after(ready, turn + 1)

            def attend_dve(a, st, layer, head, turn):
                A0 = turn * a.U
                st.begin(turn)
                if a is da:
                    v.wait_ge(a.raw, ONE + turn + 1)
                    v.wait_ge(a.perm, ONE + turn + 1)
                    st.made(v.tensor_tensor(rot, bigps[1][:, 0:L], sin, ALU.mult))
                    st.made(v.tensor_tensor(raw, raw, cos, ALU.mult))
                    st.settle()
                    st.made(v.tensor_tensor(raw, raw, rot, ALU.add))
                    st.settle()
                    st.made(v.tensor_copy(xh, raw))
                    st.settle()
                    v.tensor_tensor(xl, raw, xh.bitcast(F32), ALU.subtract).then_inc(a.parts, 1)
                    for g in range(2):
                        v.wait_ge(a.rep, ONE + turn * 4 + 2 * g + 2)
                        v.tensor_copy(KP[g], bigps[1][:, 0:L]).then_inc(a.qk, 1)
                    st.after(a.qk, turn * 2 + 2)
                else:
                    v.wait_ge(a.proj, ONE + turn + 1)
                    v.wait_ge(a.drow, turn * 32 + 32)
                    st.made(v.tensor_copy(DK[0:4], decays[0:4]))
                    st.made(v.tensor_scalar(DQ[0:4], decays[32:36], -1.0, None, ALU.mult))
                    st.made(v.tensor_scalar(QP[0][0:AW], bigps[0][0:AW, 0:L], AW ** -0.5, None, ALU.mult))
                    st.settle()
                    st.made(v.scalar_tensor_tensor(out=QP[0][AW:2 * AW], in0=bigps[0][0:AW, 0:L], scalar=AW ** -0.5,
                                                   in1=QP[0].bitcast(F32)[0:AW], op0=ALU.mult, op1=ALU.subtract))
                    v.wait_ge(a.kc, ONE + turn * 2 + 1)
                    st.made(v.tensor_tensor(KP[1][AW:2 * AW], bigps[0][AW:2 * AW, 0:L],
                                            KP[0].bitcast(F32)[AW:2 * AW], ALU.subtract))
                    v.tensor_tensor(KP[1][0:AW], bigps[0][AW:2 * AW, 0:L],
                                    KP[0].bitcast(F32)[AW:2 * AW], ALU.subtract).then_inc(a.qk, 1)
                    st.after(a.qk, turn + 1)

                at = 0 if a is da else HEADS * (AW + 1)
                v.tensor_copy(Vh, V[:, :, bass.ds(head * (AW + 1) + at, AW + 1)]).then_inc(a.vh, 1)
                for u in range(a.U):
                    c, j = divmod(u, T)
                    r, n = rows(j), META + P * j
                    v.wait_ge(a.S, ONE + A0 + u + 1)
                    v.tensor_reduce(negmax[0:r, u:u + 1], bigps[0][0:r, 0:n], AX.X, ALU.max, negate=True)\
                     .then_inc(a.max, 1)
                    st.after(a.max, A0 + u + 1)
                    st.settle()
                    st.made(v.tensor_scalar(shift[:, 0, cols(j)], ident[:, 0:r], negmax[:, u:u + 1], None, ALU.mult))
                    st.settle()
                    v.scalar_tensor_tensor(out=shift[:, 1, cols(j)], in0=ident[:, 0:r], scalar=negmax[:, u:u + 1],
                                           in1=shift.bitcast(F32)[:, 0, cols(j)], op0=ALU.mult, op1=ALU.subtract)\
                     .then_inc(a.shift, 1)
                    st.after(a.shift, A0 + u + 1)
                v.wait_ge(a.O, ONE + turn + 1)
                st.settle()
                st.made(v.reciprocal(rinv[:, 0:a.U], O[:, 0:a.U, AW]))
                st.settle()
                if a is da:
                    st.made(v.tensor_scalar(rinv[:, T:2 * T], rinv[:, T:2 * T], neglam_l[:, :], None, ALU.mult))
                    st.settle()
                    st.made(v.tensor_tensor(asq, O[:, T:2 * T, 0:AW],
                                            rinv[:, T:2 * T].unsqueeze(2).to_broadcast([P, T, AW]), ALU.mult))
                st.made(v.tensor_tensor(ah, O[:, 0:T, 0:AW], rinv[:, 0:T].unsqueeze(2).to_broadcast([P, T, AW]),
                                        ALU.mult))
                if a is da:
                    st.settle()
                    st.made(v.tensor_tensor(ah, ah, asq, ALU.add))
                squares(st, ah, asq, a.ss, turn)
                v.wait_ge(a.rstd, ONE + turn + 1)
                gains = gain_da if a is da else gain_fx
                at = 4 * HW if a is da else 4 * HW + HEADS * AW
                st.made(v.tensor_tensor(ah, ah, rstd[:, :].unsqueeze(2).to_broadcast([P, T, AW]), ALU.mult))
                st.settle()
                v.tensor_tensor(mix[:, :, bass.ds(head * AW + at, AW)], ah,
                                gains[:, bass.ds(layer, 1), :].to_broadcast([P, T, AW]), ALU.mult).then_inc(a.out, 1)
                v.wait_ge(a.out, ONE + turn + 1)
                st.end()

            with v.Fori(0, depth) as layer:
                v.wait_ge(s_gamma, layer * 32 + 16)
                for j in range(T + 1):
                    if j < T:
                        norm_apply(0, layer, j)
                    if j >= 1:
                        norm_copy(0, layer, j - 1)
                meet(v, layer, 0)

                if stop > 1:
                    v.memset(ig[:, 0, :], 0.0).then_inc(s_clean, 1)
                    v.memset(AT[:, 0, :], 0.0).then_inc(s_clean, 1)
                    v.wait_ge(s_clean, layer * CLEANS + 2)
                    wait_alone(v, h_const, layer * 32 + 32)
                    with v.Fori(0, HEADS) as head:
                        t = layer * HEADS + head
                        hg.begin(t)
                        lbc = lb[:, bass.ds(layer, 1), bass.ds(head, 1)].rearrange("p a b -> p (a b)")
                        rc = rest[:, bass.ds(layer, 1), bass.ds(head, 1)].rearrange("p a b -> p (a b)")
                        v.wait_ge(h_gexp, ONE + 2 * t + 1)
                        hg.made(v.tensor_scalar(hK, hK, 1.0, None, ALU.add))
                        hg.settle()
                        hg.made(v.reciprocal(hK, hK))
                        hg.settle()
                        hg.made(v.tensor_scalar(hX[0], hK, rc, lbc, ALU.mult, ALU.add))
                        hg.settle()
                        hg.made(v.tensor_scalar(hk, hX[0], -1.0, 1.0, ALU.mult, ALU.add))
                        hg.settle()
                        v.tensor_scalar(hX[0], hX[0], TINY, None, ALU.max).then_inc(h_clamped, 1)
                        v.wait_ge(h_gexp, ONE + 2 * t + 2)
                        hg.made(v.tensor_scalar(hQ, hQ, 1.0, None, ALU.add))
                        hg.settle()
                        hg.made(v.reciprocal(hQ, hQ))
                        hg.settle()
                        hg.made(v.scalar_tensor_tensor(out=hq, in0=bigps[0][:, 0:L], scalar=HW ** -0.5, in1=hQ,
                                                       op0=ALU.mult, op1=ALU.mult))
                        v.wait_ge(h_logf, ONE + t + 1)
                        v.tensor_tensor_scan(hG, reset, hX[1], 0.0, ALU.mult, ALU.add).then_inc(h_diff, 1)
                        hg.after(h_diff, t * 9 + 1)

                        def halves(x, li, part):
                            n = LEVELS[li]
                            lo = 0 if n < META else META
                            return x[:, lo:L].rearrange("p (b s n) -> p b s n", s=2, n=n)[:, :, part, :]

                        def differences(i):
                            X = hX[i % 2]
                            hg.settle()
                            if i <= 7:
                                li = i - 1
                                n = LEVELS[li]
                                ref = halves(hG, li, 0)[:, :, n - 1:n]
                                nb = ref.shape[1]
                                hg.made(v.tensor_tensor(halves(X, li, 0), ref.to_broadcast([P, nb, n]),
                                                        halves(hG, li, 0), ALU.subtract))
                                v.tensor_tensor(halves(X, li, 1), halves(hG, li, 1), ref.to_broadcast([P, nb, n]),
                                                ALU.subtract).then_inc(h_diff, 1)
                            else:
                                hg.made(v.tensor_tensor(X[:, 0:META], hG[:, META - 1:META].to_broadcast([P, META]),
                                                        hG[:, 0:META], ALU.subtract))
                                g3 = hG[:, META:L].rearrange("p (b n) -> p b n", n=P)
                                v.tensor_tensor(X[:, META:L].rearrange("p (b n) -> p b n", n=P),
                                                g3[:, :, P - 1:P].to_broadcast([P, T - 1, P]), g3,
                                                ALU.subtract).then_inc(h_diff, 1)
                            hg.after(h_diff, t * 9 + i + 1)

                        def factors(i):
                            X = hX[i % 2]
                            v.wait_ge(h_decay, ONE + t * 9 + i + 1)
                            if i == 0:
                                v.tensor_tensor(hQ, hq, X, ALU.mult).then_inc(h_factor, 1)
                            elif i <= 7:
                                li = i - 1
                                hg.made(v.tensor_tensor(halves(QK[:, li, :], li, 0), halves(hk, li, 0),
                                                        halves(X, li, 0), ALU.mult))
                                v.tensor_tensor(halves(QK[:, li, :], li, 1), halves(hq, li, 1),
                                                halves(X, li, 1), ALU.mult).then_inc(h_factor, 1)
                            else:
                                v.tensor_tensor(hK, hk, X, ALU.mult).then_inc(h_factor, 1)
                            hg.after(h_factor, t * 9 + i + 1)

                        for i in range(1, 10):
                            if i <= 8:
                                differences(i)
                            factors(i - 1)

                        def within(j):
                            r = rows(j)
                            v.wait_ge(h_lvl, ONE + t * T + j + 1)
                            lo = 0 if j else sum(n >= META for n in LEVELS)
                            A_ = bigps[j % 2][0:r, 0:NL * P].rearrange("p (l n) -> p l n", l=NL)[:, lo:NL, 0:r]
                            hg.made(v.tensor_tensor(A_, A_, masks[0:r, lo:NL, 0:r], ALU.mult))
                            hg.settle()
                            v.wait_ge(h_o, ONE + t * T + max(j - 1, 0))
                            v.tensor_reduce(AT[0:r, j % 2, 0:r], A_.rearrange("p l n -> p n l"), AX.X, ALU.add)\
                             .then_inc(h_at, 1)
                            hg.after(h_at, t * T + j + 1)

                        within(0)
                        v.wait_ge(h_glast, ONE + t + 1)
                        for j in range(T):
                            if j + 1 < T:
                                within(j + 1)
                            if j < T - 1:
                                v.wait_ge(h_ds, ONE + t * (T - 1) + j + 1)
                                if j == 0:
                                    v.tensor_copy(S[:, 0, :], ps[:, 7, 0:HW]).then_inc(h_S, 1)
                                else:
                                    v.wait_ge(h_S, ONE + t * (T - 1) + j)
                                    v.scalar_tensor_tensor(out=S[:, j % 2, :], in0=S[:, (j - 1) % 2, :],
                                                           scalar=glast[:, j:j + 1], in1=ps[:, 7, 0:HW],
                                                           op0=ALU.mult, op1=ALU.add).then_inc(h_S, 1)
                                hg.after(h_S, t * (T - 1) + j + 1)
                        v.wait_ge(h_oc, ONE + t * T + T)
                        squares(hg, oh, osq, h_ss, t)
                        v.wait_ge(h_eg, ONE + t * 3 + 3)
                        hg.made(v.tensor_tensor(eg, eg, ig[:, :, HW:2 * HW], ALU.mult))
                        v.wait_ge(h_rstd, ONE + t + 1)
                        hg.made(v.tensor_tensor(oh, oh, rstd[:, :].unsqueeze(2).to_broadcast([P, T, HW]), ALU.mult))
                        hg.settle()
                        hg.made(v.tensor_tensor(oh, oh, gain_hg[:, bass.ds(layer, 1), :].to_broadcast([P, T, HW]),
                                                ALU.mult))
                        hg.settle()
                        v.tensor_tensor(mix[:, :, bass.ds(head * HW, HW)], oh, eg, ALU.mult).then_inc(h_out, 1)
                        v.wait_ge(h_out, ONE + t + 1)
                        hg.end()
                    meet(v, layer, 1)

                if stop > 2:
                    wait_alone(v, v_t, layer * 64 + 64)
                    v.tensor_copy(sel, sel_read).then_inc(s_clean, 1)
                    v.wait_ge(s_clean, layer * CLEANS + 3)
                    v.tensor_copy(ident_r, ident[:, :]).then_inc(s_clean, 1)
                    v.memset(V4[:, :, :, AW:AW + 1], 1.0).then_inc(s_clean, 1)
                    v.tensor_scalar(ones_r, ident[:, :], 0.0, 1.0, ALU.mult, ALU.add).then_inc(s_clean, 1)
                    v.tensor_copy(causal_r, causal[:, :]).then_inc(s_clean, 1)
                    v.tensor_copy(neglam_l[:, :], neglam[:, bass.ds(layer, 1)]).then_inc(s_clean, 1)
                    wait_alone(v, s_clean, layer * CLEANS + 8)
                    fs.begin(layer)
                    v.wait_ge(f_p, ONE + layer + 1)
                    v.tensor_scalar(rot[0:HEADS], bigps[0][0:HEADS, 0:L], fbias[:, bass.ds(layer, 1)], None, ALU.add)\
                     .then_inc(f_x, 1)
                    v.wait_ge(f_x, ONE + layer + 1)
                    v.tensor_scalar(raw[0:HEADS], rot[0:HEADS], -1.0, 0.0, ALU.mult, ALU.max).then_inc(f_d, 1)
                    v.wait_ge(f_d, ONE + layer * 4 + 1)
                    v.wait_ge(f_l, ONE + layer + 1)
                    fs.made(v.tensor_tensor(raw[0:HEADS], raw[0:HEADS], fl, ALU.add))
                    fs.settle()
                    v.tensor_tensor_scan(fl, raw[0:HEADS], raw[0:HEADS], 0.0, ALU.add, ALU.max).then_inc(f_d, 1)
                    v.wait_ge(f_d, ONE + layer * 4 + 2)
                    v.tensor_copy(xh[0:HEADS], fl).then_inc(f_d, 1)
                    v.wait_ge(f_d, ONE + layer * 4 + 3)
                    v.tensor_tensor(xl[0:HEADS], fl, xh.bitcast(F32)[0:HEADS], ALU.subtract).then_inc(f_d, 1)
                    fs.end()
                    wait_alone(v, f_st, layer * 32 + 32)
                    with v.Fori(0, HEADS) as head:
                        attend_dve(da, das, layer, head, layer * HEADS + head)
                    meet(v, layer, 2)

                if stop > 3:
                    v.memset(decays[0:4], 1.0).then_inc(s_clean, 1)
                    v.memset(decays[32:36], -1.0).then_inc(s_clean, 1)
                    v.tensor_scalar(DQ, sin, 0.0, None, ALU.mult).then_inc(s_clean, 1)
                    v.tensor_scalar(DK, sin, 0.0, None, ALU.mult).then_inc(s_clean, 1)
                    wait_alone(v, s_clean, layer * CLEANS + 12)
                    with v.Fori(0, HEADS) as head:
                        attend_dve(fx, fxs, layer, head, layer * HEADS + head)
                    meet(v, layer, 3)

                if stop > 4:
                    def copy_mT(j):
                        v.wait_ge(p_tp, ONE + layer * 2 * T + 2 * j + 2)
                        v.wait_ge(p_mm, ONE + layer * T + max(j - 1, 0))
                        v.tensor_copy(mT[:, j % 2, 4:8, 0:rows(j)],
                                      ps[:, 7, :].rearrange("p (k n) -> p k n", k=4)[:, :, 0:rows(j)])\
                         .then_inc(p_tv, 1)

                    copy_mT(0)
                    for j in range(T):
                        r = rows(j)
                        if j + 1 < T:
                            copy_mT(j + 1)
                        v.wait_ge(p_mm, ONE + layer * T + j + 1)
                        v.tensor_tensor(h[0:r, j, :], h[0:r, j, :], bigps[j % 2][0:r, 0:D], ALU.add)\
                         .then_inc(p_h, 1)
                        norm_apply(1, layer, j)
                        if j >= 1:
                            norm_copy(1, layer, j - 1)
                    norm_copy(1, layer, T - 1)
                    meet(v, layer, 4)

                if stop > 5:
                    rs.begin(layer)

                    def do(ins):
                        rs.made(ins)
                        rs.settle()

                    def first_max(x, m, order, t_, o_, n):
                        do(v.tensor_reduce(m, x, AX.X, ALU.max))
                        do(v.tensor_tensor(t_, x, m.unsqueeze(2).to_broadcast([P, T, n]), ALU.is_ge))
                        do(v.tensor_tensor(t_, t_, order.unsqueeze(1).to_broadcast([P, T, n]), ALU.mult))
                        do(v.tensor_reduce(tm, t_, AX.X, ALU.max))
                        do(v.tensor_tensor(o_, t_, tm.unsqueeze(2).to_broadcast([P, T, n]), ALU.is_ge))

                    do(v.memset(ones, 1.0))
                    do(v.memset(lg, 0.0))
                    v.wait_ge(r_w, layer * 112 + 112)
                    v.wait_ge(r_lg, ONE + layer + 1)
                    pl = ps[:, 0, 0:T * ROUTES].rearrange("p (j e) -> p j e", j=T)
                    do(v.tensor_tensor(lg[0:META, 0, :], pl[0:META, 0, :], b_r[0:META, :], ALU.add))
                    do(v.tensor_tensor(lg[:, 1:T, :], pl[:, 1:T, :],
                                       b_r.unsqueeze(1).to_broadcast([P, T - 1, ROUTES]), ALU.add))
                    first_max(lg[:, :, 0:GROUPS], gm, first4, g4, ohg, GROUPS)
                    v.tensor_tensor(g4, lg[:, :, 0:GROUPS], gm.unsqueeze(2).to_broadcast([P, T, GROUPS]),
                                    ALU.subtract).then_inc(r_m, 1)
                    v.wait_ge(r_exp, ONE + layer * 2 + 1)
                    do(v.tensor_reduce(psel, g4, AX.X, ALU.add))
                    do(v.reciprocal(psel, psel))
                    e4 = lg[:, :, GROUPS:ROUTES].rearrange("p j (g e) -> p j g e", g=GROUPS)
                    b4 = big.rearrange("p j (g e) -> p j g e", g=GROUPS)
                    do(v.tensor_tensor(b4, e4, ohg.unsqueeze(3).to_broadcast([P, T, GROUPS, PER_GROUP]), ALU.mult))
                    do(v.tensor_reduce(ein, b4.rearrange("p j g e -> p j e g"), AX.X, ALU.add))
                    first_max(ein, m1, first8, t8, o1, PER_GROUP)
                    do(v.scalar_tensor_tensor(out=ein, in0=o1, scalar=NEG, in1=ein, op0=ALU.mult, op1=ALU.add))
                    first_max(ein, m2, first8, t8, o2, PER_GROUP)
                    v.tensor_tensor(tm, m2, m1, ALU.subtract).then_inc(r_m, 1)
                    v.wait_ge(r_exp, ONE + layer * 2 + 2)
                    do(v.tensor_scalar(m1, tm, 1.0, None, ALU.add))
                    do(v.reciprocal(m1, m1))
                    do(v.tensor_tensor(gate[:, 0, :], m1, psel, ALU.mult))
                    do(v.tensor_tensor(gate[:, 1, :], gate[:, 0, :], tm, ALU.mult))
                    do(v.tensor_tensor(ohg, ohg, valid.unsqueeze(2).to_broadcast([P, T, GROUPS]), ALU.mult))
                    for k, o in ((0, o1), (1, o2)):
                        do(v.tensor_tensor(E[k].rearrange("p j (g e) -> p j g e", g=GROUPS),
                                           ohg.unsqueeze(3).to_broadcast([P, T, GROUPS, PER_GROUP]),
                                           o.unsqueeze(2).to_broadcast([P, T, GROUPS, PER_GROUP]), ALU.mult))
                    v.tensor_tensor(both, E[0], E[1], ALU.add).then_inc(r_A, 1)
                    v.wait_ge(r_A, ONE + layer + 1)
                    v.tensor_reduce(tot, both.rearrange("p j e -> p e j"), AX.X, ALU.add).then_inc(r_tot, 1)
                    v.wait_ge(r_cnt, ONE + layer + 1)
                    do(v.tensor_scalar(cnt_i, ps[:, 2, 0:EXPERTS], float(P - 1), None, ALU.add))
                    do(v.tensor_scalar(cnt_i, cnt_i, 7, None, ALU.arith_shift_right))
                    do(v.tensor_copy(nblk, cnt_i))
                    do(v.tensor_tensor_scan(upto, nblk, nblk, 0.0, ALU.add, ALU.max))
                    do(v.tensor_tensor(base, upto, nblk, ALU.subtract))
                    do(v.tensor_scalar(base, base, float(P), None, ALU.mult))
                    v.wait_ge(r_rank, ONE + layer + 1)
                    do(v.tensor_tensor(place, ps[:, 1, 0:T * EXPERTS].rearrange("p (j e) -> p j e", j=T),
                                       base.unsqueeze(1).to_broadcast([P, T, EXPERTS]), ALU.add))
                    for k in range(2):
                        do(v.tensor_tensor(E[k], E[k], place, ALU.mult))
                        do(v.tensor_reduce(destf[:, k, :], E[k], AX.X, ALU.add))
                    v.tensor_copy(dest[:, :, :], destf).then_inc(r_dest, 1)
                    do(v.tensor_tensor(cmp[0:1], upto[0:1].unsqueeze(1).to_broadcast([1, BLOCKS, EXPERTS]),
                                       blk_no[0:1].unsqueeze(2).to_broadcast([1, BLOCKS, EXPERTS]), ALU.is_le))
                    do(v.tensor_reduce(blkf[0:1], cmp[0:1], AX.X, ALU.add))
                    do(v.tensor_scalar(blk_expert[:, :], blkf[0:1], float(EXPERTS - 1), None, ALU.min))
                    do(v.tensor_tensor(pairs_f[:, 1:2], pairs_f[:, 0:1], pairs_f[:, 1:2], ALU.add))
                    do(v.tensor_scalar(pairs[:, 0:1], upto[0:1, EXPERTS - 1:EXPERTS], 1.0, None, ALU.add))
                    do(v.tensor_scalar(pairs[:, 0:1], pairs[:, 0:1], 1, None, ALU.arith_shift_right))
                    do(v.tensor_copy(pairs_f[:, 0:1], pairs[:, 0:1]))
                    v.tensor_copy(pairs[:, 1:2], pairs_f[:, 1:2]).then_inc(r_done, 1)
                    v.wait_ge(r_done, ONE + layer + 1)
                    rs.end()
                    meet(v, layer, 5)

                if stop > 6:
                    before = v.value_load(pairs[0:1, 1:2], min_val=0, max_val=BLOCKS // 2)
                    count = v.value_load(pairs[0:1, 0:1], min_val=1, max_val=BLOCKS // 2)

                    def copy_xt(n):
                        v.wait_ge(m_xt, ONE + n)
                        v.tensor_copy(XT[:, 4:8, :].rearrange("p k n -> p (k n)"), ps[:, 6, :]).then_inc(m_xtc, 1)

                    copy_xt(before * 4 + 2 * layer + 2)
                    with v.Fori(0, count) as i:
                        t = before + i
                        for k in range(2):
                            ms.begin(t * 2 + k)
                            v.wait_ge(m_e, ONE + t * 2 + k + 1)
                            ms.made(v.tensor_scalar(sg, sg, 1.0, None, ALU.add))
                            ms.settle()
                            ms.made(v.reciprocal(sg, sg))
                            ms.settle()
                            ms.made(v.tensor_tensor(sg, ps[:, 0, :], sg, ALU.mult))
                            ms.settle()
                            for q in range(2):
                                if q == 0:
                                    v.wait_ge(m_h, ONE + t * 4 + 2 * k + 2)
                                else:
                                    v.wait_ge(m_up[k], ONE + t + 1)
                                v.wait_ge(m_gt, ONE + t * 4 + 2 * k)
                                f = slice(q * F // 2, (q + 1) * F // 2)
                                v.tensor_tensor(G[:, f], sg[:, f], ps[:, 1 + q, 0:F // 2], ALU.mult).then_inc(m_g, 1)
                            ms.end()
                            copy_xt(t * 4 + 2 * k + 2 * layer + 4)
                            v.wait_ge(m_y[k], ONE + t + 1)
                            v.wait_ge(m_out[k], 16 + t * 16)
                            v.tensor_copy(yb[:, k, 512:1024], ps[:, 4, :]).then_inc(m_yv, 1)
                    meet(v, layer, 6)

                if stop > 7:
                    cs.begin(layer)
                    for j in range(T):
                        r = rows(j)
                        v.wait_ge(c_y[j % 2], (layer * (T // 2 + 1 - j % 2) + j // 2 + 1) * 32)
                        cs.made(v.scalar_tensor_tensor(out=h[0:r, j, :], in0=ya[0:r, j % 2, 0, :],
                                                       scalar=gate[0:r, 0, j:j + 1], in1=h[0:r, j, :],
                                                       op0=ALU.mult, op1=ALU.add))
                        cs.settle()
                        v.scalar_tensor_tensor(out=h[0:r, j, :], in0=ya[0:r, j % 2, 1, :],
                                               scalar=gate[0:r, 1, j:j + 1], in1=h[0:r, j, :],
                                               op0=ALU.mult, op1=ALU.add).then_inc(c_h, 1)
                    cs.end()

            if stop >= PHASES:
                v.wait_ge(s_gamma, 32 * depth + 16)
                for j in range(1, T):
                    norm_apply(2, 0, j)


def constants():
    f = np.float32
    c = {}
    c["c_ident"] = np.eye(P, dtype=f)
    n = np.arange(P)
    c["c_earlier"] = (n[:, None] < n[None, :]).astype(f)
    c["c_causal"] = np.where(n[None, :] > n[:, None], f(NEG), f(0)).astype(f)
    masks = np.zeros((P, NL, P), f)
    for i, half in enumerate(LEVELS):
        s, t = n[:, None], n[None, :]
        masks[:, i, :] = (s // (2 * half) == t // (2 * half)) & (s % (2 * half) < half) & (t % (2 * half) >= half)
    masks[:, NL - 1, :] = np.eye(P)
    c["c_masks"] = masks
    reset = np.ones((L,), f)
    reset[0] = 0
    reset[META::P] = 0
    c["c_reset"] = reset
    inv = (f(10000.0) ** (-np.arange(0, DQK, 2, dtype=f) / f(DQK))).astype(f)
    ang = np.arange(L, dtype=f)[None, :] * inv[:, None]
    scale = np.where(n < AW, f(DQK) ** f(-0.5), f(1)).astype(f)[:, None]
    c["c_cos"] = (np.cos(ang)[n % (DQK // 2)] * scale).astype(f)
    c["c_sin"] = (np.sin(ang)[n % (DQK // 2)] * scale).astype(f)
    sel = np.zeros((P, 8, P), f)
    for g in range(2):
        for side, low in ((0, (0, 0, 1, 1)), (1, (0, 1, 0, 1))):
            for m in range(P):
                sel[side * AW + g * DQK + m % DQK, 2 * (2 * g + side) + low[m // DQK], m] = 1
    c["c_sel"] = sel
    swap = np.zeros((P, P), f)
    for m in range(P):
        if m % DQK < DQK // 2:
            swap[m + DQK // 2, m] = -1
        else:
            swap[m - DQK // 2, m] = 1
    c["c_swap"] = swap
    li = [0.8 - 0.6 * math.exp(-0.3 * l) for l in range(DEPTH)]
    c["c_lam_init"] = np.array([[x, 1.0 - x] for x in li], f)
    valid = np.ones((P, T), f)
    valid[META:, 0] = 0
    c["c_valid"] = valid
    c["c_first4"] = np.tile(np.arange(GROUPS, 0, -1, dtype=f), (P, 1))
    c["c_first8"] = np.tile(np.arange(PER_GROUP, 0, -1, dtype=f), (P, 1))
    c["c_blk_no"] = np.tile(np.arange(BLOCKS, dtype=f), (P, 1))
    return c


def layout(inputs):
    a = {k: np.ascontiguousarray(v) for k, v in inputs.items()}
    hg, at = HEADS * HW, HEADS * AW
    q0, f0, i0, g0 = 0, hg, 2 * hg, 3 * hg
    dq, dk, dv, fq, fk, fv = (4 * hg + i * at for i in range(6))
    ff = 4 * hg + 6 * at
    order = []
    for n in range(HEADS):
        for b in (f0, q0, i0, g0):
            order += list(range(b + n * HW, b + (n + 1) * HW))
    for q, k in ((dq, dk), (fq, fk)):
        for n in range(HEADS):
            for b in (q, k):
                order += list(range(b + n * AW, b + (n + 1) * AW))
    order += list(range(dv, dv + at)) + list(range(fv, fv + at)) + list(range(ff, ff + HEADS))
    a["w_in"] = np.ascontiguousarray(a["w_in"][:, :, order])
    a["w_route"] = np.concatenate([a.pop("w_group"), a.pop("w_router")], axis=2)
    a["b_route"] = np.concatenate([a.pop("b_group"), a.pop("b_router")], axis=1)
    a["hgrn_lb"] = np.ascontiguousarray(a["hgrn_lb"].reshape(DEPTH, HEADS, HW).transpose(2, 0, 1))
    a["fox_bias"] = np.ascontiguousarray(a["fox_bias"].T)
    return a


def kernel(**inputs):
    import concourse.bacc as bacc
    from concourse.bass_utils import run_bass_kernel_spmd

    arrays = layout({k: np.asarray(v) for k, v in inputs.items()})
    arrays.update(constants())
    nc = bacc.Bacc("TRN2", target_bir_lowering=False, num_devices=1)
    args = {k: nc.dram_tensor(k, v.shape, mybir.dt.from_np(v.dtype), kind="ExternalInput").ap()
            for k, v in arrays.items()}
    out = nc.dram_tensor("out", (1, SEQ, D), F32, kind="ExternalOutput").ap()
    build(nc, args, out)
    r = run_bass_kernel_spmd(nc, [arrays], core_ids=[0])
    return r.results[0]["out"]
```
